# Optimizing a Trainium2 kernel written in Bass

```python
import functools
import jax, jax.numpy as jnp
from jax import lax
import numpy as np

D_MODEL = 1024
BATCH = 1
SEQ = 512
DEPTH = 1
DEC_BATCH = 1
DEC_SEQ = 64
PAST_LEN = 512

CHUNK = 64
WINDOW = 128
WIN_CHUNKS = WINDOW // CHUNK
ATTN_HEADS = 8
ATTN_KV_HEADS = 2
ATTN_GROUP = ATTN_HEADS // ATTN_KV_HEADS
ATTN_HEAD_DIM = 64
RET_HEADS = 4
RET_KEY_DIM = 128
RET_VALUE_DIM = 256
RET_ROPE_BASE = 10000.0
FFN_HIDDEN = ((8 * D_MODEL + 3 * 256 - 1) // (3 * 256)) * 256
PLE_DIM = 256
NORM_EPS = 1e-6
GN_EPS = 1e-5
IN_SIZES = (ATTN_HEADS * ATTN_HEAD_DIM, ATTN_KV_HEADS * ATTN_HEAD_DIM, ATTN_KV_HEADS * ATTN_HEAD_DIM,
            RET_HEADS * RET_KEY_DIM, RET_HEADS * RET_KEY_DIM, RET_HEADS * RET_VALUE_DIM,
            RET_HEADS * RET_VALUE_DIM, D_MODEL, D_MODEL)
D_IN = sum(IN_SIZES)

kernel_name = 'swa_sink_retention_hybrid_stream_step'

def rmsnorm(x, g):
    xf = x.astype(jnp.float32)
    y = xf * lax.rsqrt(jnp.mean(xf * xf, axis=-1, keepdims=True) + NORM_EPS)
    return (y * g.astype(jnp.float32)).astype(x.dtype)

def split_in(z):
    parts, start = [], 0
    for size in IN_SIZES:
        parts.append(z[..., start:start + size])
        start += size
    return parts

def rotary(x, pos):
    half = x.shape[-1] // 2
    inv = 1.0 / (RET_ROPE_BASE ** jnp.linspace(0.0, 1.0, half, dtype=jnp.float32))
    ang = pos.astype(jnp.float32)[:, None] * inv[None, :]
    cos = jnp.cos(ang)[None, :, None, :]
    sin = jnp.sin(ang)[None, :, None, :]
    x1, x2 = x[..., :half], x[..., half:]
    return jnp.concatenate([x1 * cos - x2 * sin, x1 * sin + x2 * cos], axis=-1)

def ret_log_decay():
    return jnp.log1p(-jnp.exp2(-5.0 - jnp.arange(RET_HEADS, dtype=jnp.float32)))

def sink_attention(q, k, v, valid, sinks):
    s = jnp.einsum('...qhgd,...khd->...hgqk', q, k,
                   preferred_element_type=jnp.float32) * (ATTN_HEAD_DIM ** -0.5)
    if valid is not None:
        s = jnp.where(valid[..., None, None, None, :], s, -jnp.inf)
    sink = sinks.astype(jnp.float32).reshape(ATTN_KV_HEADS, ATTN_GROUP, 1, 1)
    m = jnp.maximum(jnp.max(s, axis=-1, keepdims=True), sink)
    p = jnp.exp(s - m)
    w = p / (jnp.sum(p, axis=-1, keepdims=True) + jnp.exp(sink - m))
    return jnp.einsum('...hgqk,...khd->...qhgd', w.astype(v.dtype), v)

def attention_prompt(q, k, v, sinks):
    B, S = q.shape[0], q.shape[1]
    n_chunks = S // CHUNK
    qc = q.reshape(B, n_chunks, CHUNK, ATTN_KV_HEADS, ATTN_GROUP, ATTN_HEAD_DIM)
    pad = jnp.zeros((B, WIN_CHUNKS * CHUNK, ATTN_KV_HEADS, ATTN_HEAD_DIM), k.dtype)
    kc = jnp.concatenate([pad, k], axis=1).reshape(B, n_chunks + WIN_CHUNKS, CHUNK, ATTN_KV_HEADS, ATTN_HEAD_DIM)
    vc = jnp.concatenate([pad, v], axis=1).reshape(B, n_chunks + WIN_CHUNKS, CHUNK, ATTN_KV_HEADS, ATTN_HEAD_DIM)
    kb = jnp.concatenate([kc[:, j:j + n_chunks] for j in range(WIN_CHUNKS + 1)], axis=2)
    vb = jnp.concatenate([vc[:, j:j + n_chunks] for j in range(WIN_CHUNKS + 1)], axis=2)
    seg_chunk = jnp.arange(n_chunks)[:, None] + jnp.arange(WIN_CHUNKS + 1)[None, :] - WIN_CHUNKS
    valid = jnp.repeat(seg_chunk >= 0, CHUNK, axis=1)[None]
    o = sink_attention(qc, kb, vb, valid, sinks)
    o = o.reshape(B, S, ATTN_KV_HEADS, ATTN_GROUP, ATTN_HEAD_DIM)
    return o, k[:, -WINDOW:], v[:, -WINDOW:]

def attention_sample(q, k, v, sinks, cache_k, cache_v):
    n_win = cache_k.shape[1]
    kf = jnp.concatenate([cache_k.astype(k.dtype), k], axis=1)
    vf = jnp.concatenate([cache_v.astype(v.dtype), v], axis=1)
    o = sink_attention(q, kf, vf, None, sinks)
    return o, kf[:, -n_win:], vf[:, -n_win:]

def retention_block(state, q, k, v, log_g):
    L = q.shape[1]
    n = jnp.arange(L, dtype=jnp.float32)
    diff = n[:, None] - n[None, :]
    decay = jnp.where(diff >= 0, jnp.exp(log_g[:, None, None] * jnp.maximum(diff, 0.0)), 0.0)
    s = jnp.einsum('blhd,bmhd->bhlm', q, k) * decay
    intra = jnp.einsum('bhlm,bmhe->blhe', s, v)
    cross = jnp.einsum('blhd,bhde->blhe', q, state) * jnp.exp(log_g[None, :] * (n[:, None] + 1.0))[None, :, :, None]
    k_dec = jnp.exp(log_g[None, :] * (float(L) - 1.0 - n[:, None]))
    new_state = (jnp.exp(log_g * float(L))[None, :, None, None] * state
                 + jnp.einsum('blhd,blhe,lh->bhde', k, v, k_dec))
    return new_state, intra + cross

def retention_prompt(q, k, v):
    B, S, H = q.shape[0], q.shape[1], q.shape[2]
    n_chunks = S // CHUNK
    log_g = ret_log_decay()

    def to_chunks(t):
        return t.reshape(B, n_chunks, CHUNK, H, t.shape[-1]).swapaxes(0, 1)

    def step(st, xs):
        return retention_block(st, xs[0], xs[1], xs[2], log_g)

    state0 = jnp.zeros((B, H, RET_KEY_DIM, RET_VALUE_DIM), jnp.float32)
    state, o = lax.scan(step, state0, (to_chunks(q), to_chunks(k), to_chunks(v)))
    return o.swapaxes(0, 1).reshape(B, S, H, RET_VALUE_DIM), state

def retention_sample(q, k, v, state0):
    state, o = retention_block(state0.astype(jnp.float32), q, k, v, ret_log_decay())
    return o, state

def head_group_norm(o):
    mu = jnp.mean(o, axis=-1, keepdims=True)
    var = jnp.mean(jnp.square(o - mu), axis=-1, keepdims=True)
    return (o - mu) * lax.rsqrt(var + GN_EPS)

def layer(x, p, pos, attend, retain, g_mix_pre, w_in, attn_sinks, w_branch_attn, w_branch_ret,
          w_out, g_mix_post, g_ffn_pre, w_ffn_gate, w_ffn_up, w_ffn_down, g_ffn_post,
          w_ple_proj, w_ple_gate):
    B, L = x.shape[0], x.shape[1]
    h = rmsnorm(x, g_mix_pre)
    q_a, k_a, v_a, q_r, k_r, v_r, g_r, gate_a, gate_r = split_in(h @ w_in)
    o_a, k_state, v_state = attend(
        q_a.reshape(B, L, ATTN_KV_HEADS, ATTN_GROUP, ATTN_HEAD_DIM),
        k_a.reshape(B, L, ATTN_KV_HEADS, ATTN_HEAD_DIM),
        v_a.reshape(B, L, ATTN_KV_HEADS, ATTN_HEAD_DIM), attn_sinks)
    qr = rotary(q_r.reshape(B, L, RET_HEADS, RET_KEY_DIM).astype(jnp.float32), pos)
    kr = rotary(k_r.reshape(B, L, RET_HEADS, RET_KEY_DIM).astype(jnp.float32), pos) * (RET_KEY_DIM ** -0.5)
    vr = v_r.reshape(B, L, RET_HEADS, RET_VALUE_DIM).astype(jnp.float32)
    o_r, ret_state = retain(qr, kr, vr)
    o_r = head_group_norm(o_r).reshape(B, L, RET_HEADS * RET_VALUE_DIM).astype(x.dtype) * jax.nn.silu(g_r)
    merged = (jax.nn.sigmoid(gate_a) * (o_a.reshape(B, L, -1) @ w_branch_attn)
              + jax.nn.sigmoid(gate_r) * (o_r @ w_branch_ret))
    x = x + rmsnorm(merged @ w_out, g_mix_post)
    h = rmsnorm(x, g_ffn_pre)
    f = (jax.nn.silu(h @ w_ffn_gate) * (h @ w_ffn_up)) @ w_ffn_down
    x = x + rmsnorm(f, g_ffn_post)
    x = x + (p @ w_ple_proj) * jax.nn.sigmoid(x @ w_ple_gate)
    return x, k_state, v_state, ret_state

def setup_inputs(seed: int = 0) -> dict:
    key = jax.random.key(seed)
    ks = jax.random.split(key, 24)
    f32 = jnp.float32
    n_win = min(WINDOW, PAST_LEN)

    def nrm(k, shape, scale):
        return jax.random.normal(k, shape, f32) * scale

    def gain(k):
        return 1.0 + nrm(k, (DEPTH, D_MODEL), 0.01)

    return {
        'x_prompt': nrm(ks[0], (BATCH, SEQ, D_MODEL), 1.0),
        'x_sample': nrm(ks[1], (DEC_BATCH, DEC_SEQ, D_MODEL), 1.0),
        'p_prompt': nrm(ks[2], (DEPTH, BATCH, SEQ, PLE_DIM), 1.0),
        'p_sample': nrm(ks[3], (DEPTH, DEC_BATCH, DEC_SEQ, PLE_DIM), 1.0),
        'cache_attn_k': nrm(ks[4], (DEPTH, DEC_BATCH, n_win, ATTN_KV_HEADS, ATTN_HEAD_DIM), 1.0),
        'cache_attn_v': nrm(ks[5], (DEPTH, DEC_BATCH, n_win, ATTN_KV_HEADS, ATTN_HEAD_DIM), 1.0),
        'state_ret': nrm(ks[6], (DEPTH, DEC_BATCH, RET_HEADS, RET_KEY_DIM, RET_VALUE_DIM), 0.5),
        'g_mix_pre': gain(ks[7]),
        'w_in': nrm(ks[8], (DEPTH, D_MODEL, D_IN), D_MODEL ** -0.5),
        'attn_sinks': nrm(ks[9], (DEPTH, ATTN_HEADS), 1.0),
        'w_branch_attn': nrm(ks[10], (DEPTH, ATTN_HEADS * ATTN_HEAD_DIM, D_MODEL), (ATTN_HEADS * ATTN_HEAD_DIM) ** -0.5),
        'w_branch_ret': nrm(ks[11], (DEPTH, RET_HEADS * RET_VALUE_DIM, D_MODEL), (RET_HEADS * RET_VALUE_DIM) ** -0.5),
        'w_out': nrm(ks[12], (DEPTH, D_MODEL, D_MODEL), D_MODEL ** -0.5),
        'g_mix_post': gain(ks[13]),
        'g_ffn_pre': gain(ks[14]),
        'w_ffn_gate': nrm(ks[15], (DEPTH, D_MODEL, FFN_HIDDEN), D_MODEL ** -0.5),
        'w_ffn_up': nrm(ks[16], (DEPTH, D_MODEL, FFN_HIDDEN), D_MODEL ** -0.5),
        'w_ffn_down': nrm(ks[17], (DEPTH, FFN_HIDDEN, D_MODEL), FFN_HIDDEN ** -0.5),
        'g_ffn_post': gain(ks[18]),
        'w_ple_proj': nrm(ks[19], (DEPTH, PLE_DIM, D_MODEL), PLE_DIM ** -0.5),
        'w_ple_gate': nrm(ks[20], (DEPTH, D_MODEL, D_MODEL), D_MODEL ** -0.5),
    }

def reference(x_prompt, x_sample, p_prompt, p_sample, cache_attn_k, cache_attn_v, state_ret,
              g_mix_pre, w_in, attn_sinks, w_branch_attn, w_branch_ret, w_out, g_mix_post,
              g_ffn_pre, w_ffn_gate, w_ffn_up, w_ffn_down, g_ffn_post, w_ple_proj, w_ple_gate):
    pos_prompt = jnp.arange(x_prompt.shape[1])
    pos_sample = PAST_LEN + jnp.arange(x_sample.shape[1])
    y_p, y_s = x_prompt, x_sample
    kp_l, vp_l, rp_l, ks_l, vs_l, rs_l = [], [], [], [], [], []
    for i in range(DEPTH):
        w_i = (g_mix_pre[i], w_in[i], attn_sinks[i], w_branch_attn[i], w_branch_ret[i], w_out[i],
               g_mix_post[i], g_ffn_pre[i], w_ffn_gate[i], w_ffn_up[i], w_ffn_down[i], g_ffn_post[i],
               w_ple_proj[i], w_ple_gate[i])
        y_p, kp, vp, rp = layer(y_p, p_prompt[i], pos_prompt, attention_prompt, retention_prompt, *w_i)
        y_s, ksm, vsm, rsm = layer(
            y_s, p_sample[i], pos_sample,
            functools.partial(attention_sample, cache_k=cache_attn_k[i], cache_v=cache_attn_v[i]),
            functools.partial(retention_sample, state0=state_ret[i]), *w_i)
        kp_l.append(kp); vp_l.append(vp); rp_l.append(rp.astype(x_prompt.dtype))
        ks_l.append(ksm); vs_l.append(vsm); rs_l.append(rsm.astype(x_sample.dtype))
    return (y_p, y_s, jnp.stack(kp_l), jnp.stack(vp_l), jnp.stack(rp_l),
            jnp.stack(ks_l), jnp.stack(vs_l), jnp.stack(rs_l))


_drawn_inputs = setup_inputs


def setup_inputs(seed=0):
    import zlib

    import numpy as np

    out = dict(_drawn_inputs(seed))
    spreads = {}
    factors = {'g_mix_pre': 3.462,
     'attn_sinks': 8.0,
     'g_mix_post': 6.909,
     'g_ffn_pre': 7.156,
     'g_ffn_post': 8.0}
    for name, (base, spread) in spreads.items():
        noise = np.random.default_rng([zlib.crc32(name.encode()), seed]).standard_normal(out[name].shape)
        drawn = base * np.exp(spread * noise) if base else spread * noise
        out[name] = __import__('jax').numpy.asarray(drawn.astype(out[name].dtype))
    for name, factor in factors.items():
        out[name] = (out[name] * factor).astype(out[name].dtype)
    return out
```

```python
from contextlib import ExitStack

import numpy as np
import concourse.bass as bass
from concourse import mybir

F32 = mybir.dt.float32
F32R = mybir.dt.float32r
ALU = mybir.AluOpType
ACT = mybir.ActivationFunctionType
AX_X = mybir.AxisListType.X

P = 128
D = 1024
SEQ, DEC, PAST = 512, 64, 512
ROWS = SEQ + DEC
HALF = ROWS // 2
PADROWS = ROWS + 64
RT = PADROWS // P
KD = D // P
HEADS, KV, HD = 8, 2, 64
GROUP = HEADS // KV
KW = 2 * P
RH, RK, RV = 4, 128, 256
EV = RV // P
FFN = 2816
FT = FFN // P
FTH = FT // 2
PLE = 256
KP = PLE // P
EPS, GN_EPS = 1e-6, 1e-5
SCALE = float(HD) ** -0.5

C_QA = 0
C_KA = C_QA + HEADS * HD
C_VA = C_KA + KV * HD
C_QR = C_VA + KV * HD
C_KR = C_QR + RH * RK
C_VR = C_KR + RH * RK
C_GR = C_VR + RH * RV
C_GA = C_GR + RH * RV
C_GB = C_GA + D

U_KV, J_KV = 0, 0
U_Q, J_Q = 2, 2
U_HEAD, J_HEAD = 6, 6
U_GATE, J_GATE = U_HEAD + 6 * RH, J_HEAD + 6 * RH
U_MRG, J_MRG = U_GATE + 8, J_GATE + 8
U_MRG2, J_MRG2 = U_MRG + 16, J_MRG + 16
U_OUT, J_OUT = U_MRG2 + 8, J_MRG2 + 8
U_P0, J_P0 = U_OUT + KD, J_OUT + KD
U_FA, J_FA = U_P0 + 1, J_P0 + 4
U_DA, J_DA = U_FA + 2 * FTH, J_FA + 2 * FTH
U_FB, J_FB = U_DA + 2 * KD, J_DA + KD
U_DB, J_DB = U_FB + 2 * FTH, J_FB + 2 * FTH
U_P1, J_P1 = U_DB + 2 * KD, J_DB + KD
U_PG, J_PG = U_P1 + 1, J_P1 + 4
U_END = U_PG + KD
DOWN_K = (6, 5)

T_ID = 0
T_DEC = T_ID + P
T_QD = T_DEC + RH * P
T_KD = T_QD + RH * P
T_KDS = T_KD + RH
T_GL = T_KDS + RH
T_GLS = T_GL + RH
T_MASK = T_GLS + RH
T_COLS = T_MASK + 3 * KW
T_ROT = T_COLS
T_ALL = T_ROT + 2 * ROWS

MASKED = -1.0e30


def tables():
    t = np.zeros((P, T_ALL), np.float32)
    t[:, T_ID:T_ID + P] = np.eye(P)
    m = np.arange(P, dtype=np.float64)
    for h in range(RH):
        lg = np.log1p(-np.exp2(-5.0 - h))
        diff = m[None, :] - m[:, None]
        t[:, T_DEC + h * P:T_DEC + (h + 1) * P] = np.where(
            diff >= 0, np.exp(lg * np.maximum(diff, 0)), 0.0) * RK ** -0.5
        t[:, T_QD + h * P:T_QD + (h + 1) * P] = np.exp(lg * (m + 1))[None, :]
        t[:, T_KD + h] = np.exp(lg * (P - 1 - m)) * RK ** -0.5
        t[:, T_KDS + h] = np.where(m < DEC, np.exp(lg * np.maximum(DEC - 1 - m, 0)), 0.0) * RK ** -0.5
        t[:, T_GL + h] = np.exp(lg * P)
        t[:, T_GLS + h] = np.exp(lg * DEC)
    k = np.arange(KW)[None, :]
    late = np.arange(P)[:, None] >= 64
    own = np.where(late, k >= 64, k < 192)
    t[:, T_MASK:T_MASK + KW] = np.where(own & (k >= P), 0.0, MASKED)
    t[:, T_MASK + KW:T_MASK + 2 * KW] = np.where(own, 0.0, MASKED)
    t[:, T_MASK + 2 * KW:T_MASK + 3 * KW] = np.where(k < P + DEC, 0.0, MASKED)
    half = RK // 2
    inv = (1.0 / (np.float32(10000.0) ** np.linspace(0.0, 1.0, half, dtype=np.float32))).astype(np.float32)
    ang = (np.arange(ROWS, dtype=np.float32)[None, :] * inv[:, None]).astype(np.float32)
    cos, sin = np.cos(ang.astype(np.float64)), np.sin(ang.astype(np.float64))
    t[:, T_ROT:T_ROT + ROWS] = np.concatenate([cos, cos])
    t[:, T_ROT + ROWS:T_ALL] = np.concatenate([-sin, sin])
    return t


def unit(base, step=0, i=0):
    return base // 2 + (step // 2) * i, base % 2


def span(start, size):
    return slice(start, start + size) if isinstance(start, int) else bass.ds(start, size)


def wait(eng, sem, value):
    if not (isinstance(value, int) and value <= 0):
        eng.wait_ge(sem, value)


PLACES = [
    [("att", "A", 0), ("ret", "A", 0)],
    [("att", "N", 0)],
    [("ret", "B", 0), ("ret", "A", 1), ("ret", "N", 0)],
    [("ret", "C", 0), ("att", "B", 0)],
    [("att", "C", 0), ("ret", "B", 1), ("ret", "A", 2), ("ret", "N", 1)],
    [("ret", "C", 1), ("att", "A", 1)],
    [("ret", "B", 2), ("ret", "A", 3), ("ret", "N", 2)],
    [("ret", "C", 2), ("att", "N", 1)],
    [("att", "B", 1), ("ret", "B", 3), ("ret", "A", 4), ("ret", "N", 3)],
    [("ret", "C", 3), ("att", "C", 1)],
    [("ret", "B", 4), ("ret", "N", 4), ("v", None, 0)],
    [("ret", "C", 4), ("v", None, 1)],
]


def earlier_use(c):
    return 1 if c == 0 else 2


def encoder_layer(nc, x_p, x_s, p_p, p_s, cache_k, cache_v, state_in, g_mix_pre, w_in, sinks_in,
                  w_ba, w_br, w_out, g_mix_post, g_ffn_pre, w_fg, w_fu, w_fd, g_ffn_post, w_pp, w_pg,
                  table_in, scratch, y_p, y_s, k_p, v_p, r_p, k_s, v_s, r_s):
    with ExitStack() as ctx:
        base = (nc.sbuf_base + 63) // 64 * 64
        cursor = [base]

        def place(name, shape, dt=F32, at=None):
            size = int(np.prod(shape[1:])) * 4
            if at is None:
                at = cursor[0]
                cursor[0] += (size + 31) // 32 * 32
            assert at + size <= nc.sbuf_usable_end, (name, at + size, nc.sbuf_usable_end)
            return nc.alloc_sbuf_tensor_at(name, shape, dt, offset=at)

        def sem(name):
            return ctx.enter_context(nc.semaphore(name))

        tab = place("tab", [P, T_COLS])
        rot = place("rot", [P, 2, ROWS])
        ident = tab[:, T_ID:T_ID + P]
        gains = place("gains", [P, 4 * KD])
        ones = place("ones", [P, P])
        sinks = place("sinks", [P, HEADS])
        raw = place("raw", [P, 2, KD * P])
        whi = place("whi", [P, 2, KD * P], F32R)
        wlo = place("wlo", [P, 2, KD * P], F32R)
        rb = place("rb", [P, ROWS])
        zt = place("zt", [P, 2, ROWS])
        ta = place("ta", [P, ROWS])
        tb = place("tb", [P, ROWS])
        ph = place("ph", [P, KP, ROWS], F32R)
        pl = place("pl", [P, KP, ROWS], F32R)
        rowsum = place("rowsum", [P, 8])
        rowvar = place("rowvar", [P, 8])
        rstd = place("rstd", [P, 8])
        neg_half = place("neg_half", [P, 8])
        slab = KD * ROWS * 4
        a_at, b_at, c_at, d_at = (cursor[0] + n * slab for n in range(4))
        e_at = d_at + slab
        f_at = e_at + slab // 2
        xh = place("xh", [P, KD, ROWS], F32R, at=a_at)
        xl = place("xl", [P, KD, ROWS], F32R, at=b_at)
        o_ret = place("o_ret", [P, KD, ROWS], at=c_at)
        sig = place("sig", [P, 4, 2, ROWS], at=d_at)
        o_att = place("o_att", [P, GROUP, ROWS], at=e_at)
        x_t = place("x_t", [P, KD, ROWS], at=d_at)
        x_row = place("x_row", [P, RT, D], at=e_at)
        p_row = place("p_row", [P, RT, PLE], at=c_at)
        g_row = place("g_row", [4 * KD, P], at=c_at + RT * PLE * 4)
        sink_row = place("sink_row", [1, HEADS], at=c_at + RT * PLE * 4 + 4 * P)
        square = place("square", [P, D], at=c_at + RT * PLE * 4 + 4 * P + 64)
        cursor[0] = f_at
        qt = place("qt", [P, GROUP, PADROWS])
        kt = place("kt", [P, P + PADROWS])
        ckt = place("ckt", [P, P])
        va = place("va", [P, RT + 1, P])
        cva = place("cva", [P, P])
        ck_row = place("ck_row", [P, P])
        k_row = place("k_row", [P, 2, P])
        q_st = place("q_st", [P, GROUP, P])
        k_st = place("k_st", [P, KW])
        v_st = place("v_st", [P, 2, P])
        prob = place("prob", [P, GROUP, KW])
        prob_t = place("prob_t", [P, 2, GROUP * P])
        top = place("top", [P, GROUP])
        neg_top = place("neg_top", [P, GROUP])
        den = place("den", [P, GROUP])
        sink_exp = place("sink_exp", [P, GROUP])
        qr = place("qr", [P, 2, PADROWS])
        kr = place("kr", [P, 2, PADROWS])
        vr = place("vr", [P, 2, RT, RV])
        gr = place("gr", [P, 2, EV, ROWS])
        rk_st = place("rk_st", [P, 2, P])
        q_dec = place("q_dec", [P, 2, P])
        s_dec = place("s_dec", [P, 2, P])
        k_dec = place("k_dec", [P, 2, P])
        o_norm = place("o_norm", [P, 2, RV])
        state_p = place("state_p", [P, RV])
        state_s = place("state_s", [P, RV])
        stats = place("stats", [P, 8])
        moments = place("moments", [P, 2])
        grstd = place("grstd", [P, 1])
        work_end = cursor[0]
        split_at = (nc.sbuf_usable_end - 3 * slab) // 32 * 32
        assert split_at >= e_at + slab
        ah = place("ah", [P, GROUP, ROWS], F32R, at=split_at)
        al = place("al", [P, GROUP, ROWS], F32R, at=split_at + slab // 2)
        rh = place("rh", [P, KD, ROWS], F32R, at=split_at + slab)
        rl = place("rl", [P, KD, ROWS], F32R, at=split_at + 2 * slab)
        yh = place("yh", [P, KD, ROWS], F32R, at=c_at)
        ml = place("ml", [P, KD, ROWS], F32R, at=e_at)
        yl = place("yl", [P, KD, ROWS], F32R, at=d_at)
        wide = place("wide", [P, KD, ROWS], at=a_at)
        res = place("res", [P, KD, ROWS], at=b_at)
        proj = place("proj", [P, KD, ROWS], at=e_at)
        cursor[0] = e_at + slab
        fh = place("fh", [P, FTH, ROWS], F32R)
        fl = place("fl", [P, FTH, ROWS], F32R)
        sqacc = place("sqacc", [P, PADROWS])
        cursor[0] = e_at + slab
        yt = place("yt", [P, 2, ROWS])
        y_row = place("y_row", [P, 2, RT, P])
        mb = place("mb", [P, ROWS], at=e_at + slab)
        assert e_at + slab + ROWS * 4 <= split_at
        diag = tb

        acc = ctx.enter_context(nc.psum_tensor("acc", [P, 2, 2, 512], F32))
        small = ctx.enter_context(nc.psum_tensor("small", [P, 2048], F32))
        att = small[:, 0:1024]
        ret_s, ret_kt, ret_ot = small[:, 1024:1152], small[:, 1152:1280], small[:, 1280:1536]
        ret_o, ret_dl = small[:, 1536:1792], small[:, 1792:2048]

        tables_in = sem("tables_in")
        gains_in = sem("gains_in")
        x_in = [sem(f"x_in{r}") for r in range(RT)]
        p_in = sem("p_in")
        cache_in = sem("cache_in")
        loaded = [sem("loaded0"), sem("loaded1")]
        hi_ready, lo_ready, unit_done = sem("hi_ready"), sem("lo_ready"), sem("unit_done")
        acc_free = [sem("acc_free0"), sem("acc_free1")]
        gate_sig = [sem("gate_sig0"), sem("gate_sig1")]
        ple_done = sem("ple_done")
        init_done = sem("init_done")
        gain_t, gain_ready = sem("gain_t"), sem("gain_ready")
        xt_psum, xt_copied, xh_ready, xl_ready = sem("xt_psum"), sem("xt_copied"), sem("xh_ready"), sem("xl_ready")
        x_saved, x_back = sem("x_saved"), sem("x_back")
        squares_ready, var_ready, rstd_ready, diag_ready = (
            sem("squares_ready"), sem("var_ready"), sem("rstd_ready"), sem("diag_ready"))
        bcast_done, rb_ready, sums_done = sem("bcast_done"), sem("rb_ready"), sem("sums_done")
        kt_ready, va_ready, kv_t, va_rows, kv_rows, ckt_ready = (
            sem("kt_ready"), sem("va_ready"), sem("kv_t"), sem("va_rows"), sem("kv_rows"), sem("ckt_ready"))
        swap_ready, cos_ready, rotated = sem("swap_ready"), sem("cos_ready"), sem("rotated")
        v_t, v_rows = sem("v_t"), sem("v_rows")
        sg_ready, g_ready = sem("sg_ready"), sem("g_ready")
        att_staged, cache_staged, att_score, att_top, att_exp, att_den, att_prob, att_t = (
            sem("att_staged"), sem("cache_staged"), sem("att_score"), sem("att_top"), sem("att_exp"), sem("att_den"),
            sem("att_prob"), sem("att_t"))
        att_t0, att_t1, att_pv, att_out = sem("att_t0"), sem("att_t1"), sem("att_pv"), sem("att_out")
        ret_kst, ret_qd, ret_A, ret_sd, ret_kd = (
            sem("ret_kst"), sem("ret_qd"), sem("ret_A"), sem("ret_sd"), sem("ret_kd"))
        ret_B, ret_state, ret_mom, ret_grstd, ret_norm, ret_C, ret_gated = (
            sem("ret_B"), sem("ret_state"), sem("ret_mom"), sem("ret_grstd"), sem("ret_norm"),
            sem("ret_C"), sem("ret_gated"))
        state_in_s, state_p_out, state_s_out = sem("state_in_s"), sem("state_p_out"), sem("state_s_out")
        branch_hi, branch_lo = sem("branch_hi"), sem("branch_lo")
        m_ready, m_hi, m_lo = sem("m_ready"), sem("m_hi"), sem("m_lo")
        sq_ready, sq_added = sem("sq_ready"), sem("sq_added")
        ph_ready, pl_ready = sem("ph_ready"), sem("pl_ready")
        scaled, res_ready, y_hi, y_lo = sem("scaled"), sem("res_ready"), sem("y_hi"), sem("y_lo")
        silu_sg, silu_ready, f_ready, f_hi, f_lo = (
            sem("silu_sg"), sem("silu_ready"), sem("f_ready"), sem("f_hi"), sem("f_lo"))
        y_ready, y_t, y_rows = sem("y_ready"), sem("y_t"), sem("y_rows")
        y_out = [sem("y_out0"), sem("y_out1")]
        out_done = sem("out_done")
        dve_top, dve_rot, dve_ret, dve_y = sem("dve_top"), sem("dve_rot"), sem("dve_ret"), sem("dve_y")

        act_passed, dve_passed, pool_passed = sem("act_passed"), sem("dve_passed"), sem("pool_passed")

        CREDIT = 1

        wi = w_in[0].rearrange("(k p) n -> p k n", p=P)
        wba_v = [w_ba[0][n * 256:(n + 1) * 256, :].rearrange("(j p) n -> p j n", p=HD) for n in range(2)]
        wbr_v = w_br[0].rearrange("(k p) n -> p k n", p=P)
        wo_v = w_out[0].rearrange("(k p) n -> p k n", p=P)
        wfg_v = w_fg[0].rearrange("(k p) n -> p k n", p=P)
        wfu_v = w_fu[0].rearrange("(k p) n -> p k n", p=P)
        wfd_v = w_fd[0].rearrange("(k p) n -> p k n", p=P)
        wpp_v = w_pp[0].rearrange("(k p) n -> p k n", p=P)
        wpg_v = w_pg[0].rearrange("(k p) n -> p k n", p=P)

        def acc_of(a):
            return acc[:, a, :, 0:HALF]

        def halves(ap):
            return ap.rearrange("p (h n) -> p h n", h=2)

        block = ctx.enter_context(nc.Block())

        @block.sync
        def _(sp):
            def load(vs, parts):
                v, s = vs
                wait(sp, lo_ready, 2 * v + s - 1)
                assert len(parts) == 2
                for dst, src in parts:
                    sp.dma_start(dst, src).then_inc(loaded[s], 16)

            def columns(vs, view, col, k0=0, ks=KD):
                first = (ks + 1) // 2
                s = vs[1]
                slot = raw[:, s, :].rearrange("p (k n) -> p k n", n=P)
                load(vs, [(slot[:, 0:first, :], view[:, k0:k0 + first, span(col, P)]),
                          (slot[:, first:ks, :], view[:, k0 + first:k0 + ks, span(col, P)])])

            def q_columns(vs, j):
                slot = raw[:, vs[1], :].rearrange("p (k n) -> p k n", n=P)
                load(vs, [(slot[:, :, 0:HD], wi[:, :, span(C_QA + HD * j, HD)]),
                          (slot[:, :, HD:P], wi[:, :, span(C_QA + HD * (j + GROUP), HD)])])

            def att_columns(vs, col):
                slot = raw[:, vs[1], 0:GROUP * P].rearrange("p (k n) -> p k n", n=P)
                load(vs, [(slot[64 * n:64 * n + 64], wba_v[n][:, :, span(col, P)]) for n in range(2)])

            def ple_columns(vs, n):
                slot = raw[:, vs[1], :].rearrange("p (k n) -> p k n", n=4 * P)
                load(vs, [(slot[:, k, :], wpp_v[:, k, n * 4 * P:(n + 1) * 4 * P]) for k in range(KP)])

            for r in range(RT):
                if r < RT - 1:
                    sp.dma_start(x_row[:, r, :], x_p[0, r * P:(r + 1) * P, :]).then_inc(x_in[r], 16)
                else:
                    sp.dma_start(x_row[0:DEC, r, :], x_s[0]).then_inc(x_in[r], 16)
            columns(unit(U_KV), wi, C_KA)
            columns(unit(U_KV + 1), wi, C_VA)
            with sp.Fori(0, GROUP // 2) as i:
                for n in range(2):
                    q_columns(unit(U_Q + n, 2, i), 2 * i + n)
            with sp.Fori(0, RH) as h:
                for n, col in enumerate((C_QR + RK * h, C_GR + RV * h, C_KR + RK * h,
                                         C_VR + RV * h, C_VR + RV * h + P, C_GR + RV * h + P)):
                    columns(unit(U_HEAD + n, 6, h), wi, col)
            with sp.Fori(0, 4) as c:
                columns(unit(U_GATE, 2, c), wi, C_GA + P * c)
                columns(unit(U_GATE + 1, 2, c), wi, C_GB + P * c)
            with sp.Fori(0, 4) as c:
                att_columns(unit(U_MRG, 4, c), P * c)
                columns(unit(U_MRG + 1, 4, c), wbr_v, P * c)
                columns(unit(U_MRG + 2, 4, c), wi, C_GA + 4 * P + P * c)
                columns(unit(U_MRG + 3, 4, c), wi, C_GB + 4 * P + P * c)
            with sp.Fori(0, 4) as c:
                att_columns(unit(U_MRG2, 2, c), 4 * P + P * c)
                columns(unit(U_MRG2 + 1, 2, c), wbr_v, 4 * P + P * c)
            with sp.Fori(0, KD // 2) as i:
                for n in range(2):
                    columns(unit(U_OUT + n, 2, i), wo_v, 2 * P * i + n * P)
            ple_columns(unit(U_P0), 0)
            for half, (uf, ud) in enumerate(((U_FA, U_DA), (U_FB, U_DB))):
                with sp.Fori(0, FTH) as i:
                    columns(unit(uf, 2, i), wfg_v, half * FTH * P + P * i)
                    columns(unit(uf + 1, 2, i), wfu_v, half * FTH * P + P * i)
                with sp.Fori(0, KD) as c:
                    columns(unit(ud, 2, c), wfd_v, P * c, k0=half * FTH, ks=DOWN_K[0])
                    columns(unit(ud + 1, 2, c), wfd_v, P * c, k0=half * FTH + DOWN_K[0], ks=DOWN_K[1])
            ple_columns(unit(U_P1), 1)
            with sp.Fori(0, KD // 2) as i:
                for n in range(2):
                    columns(unit(U_PG + n, 2, i), wpg_v, 2 * P * i + n * P)
            for c in range(KD):
                sp.wait_ge(y_rows, c + 1)
                sp.dma_start(y_p[0].rearrange("(r p) n -> p r n", p=P)[:, :, c * P:(c + 1) * P],
                             y_row[:, c % 2, 0:RT - 1, :]).then_inc(y_out[c % 2], 16)
                sp.dma_start(y_s[0][:, c * P:(c + 1) * P], y_row[0:DEC, c % 2, RT - 1, :]).then_inc(y_out[c % 2], 16)
            for n in range(2):
                sp.wait_ge(y_out[n], 32 * KD // 2)

        @block.tensor
        def _(pe):
            def products(s, a, ks, rhs_h, rhs_l, first, last, tile_at):
                ins = None
                for n, k in enumerate(ks):
                    at = tile_at(k)
                    for m, (w, x) in enumerate(((whi, rhs_h), (whi, rhs_l), (wlo, rhs_h))):
                        for hf in range(2):
                            ins = nc.tensor.matmul(
                                acc[:, a, hf, 0:HALF], w[:, s, at:at + P], x(k)[:, hf * HALF:(hf + 1) * HALF],
                                start=first and n == 0 and m == 0, stop=last and n == len(ks) - 1 and m == 2)
                return ins

            def run_unit(vs, wa, rhs, ks=KD, k0=0, first=True, last=True, ready=None,
                         between=None):
                (v, s), (w, a) = vs, wa
                if first:
                    wait(pe, acc_free[a], w)
                pe.wait_ge(lo_ready, 2 * v + s + 1)
                rh_, rl_ = rhs
                if between is not None:
                    for part in (range(ks // 2), range(ks // 2, ks)):
                        ins = products(s, a, part, lambda k: rh_[:, k, :], lambda k: rl_[:, k, :],
                                       part[0] == 0, part[-1] == ks - 1, lambda k: k * P)
                        if part[0] == 0:
                            between()
                elif ready is None:
                    ins = products(s, a, range(ks), lambda k: rh_[:, k0 + k, :], lambda k: rl_[:, k0 + k, :],
                                   first, last, lambda k: k * P)
                else:
                    for k in range(ks):
                        ready(k0 + k)
                        ins = products(s, a, [k], lambda k: rh_[:, k0 + k, :], lambda k: rl_[:, k0 + k, :],
                                       first and k == 0, last and k == ks - 1, lambda k: k * P)
                ins.then_inc(unit_done, 1)

            def run_ple(u, j, n):
                v, s = unit(u)
                pe.wait_ge(lo_ready, 2 * v + s + 1)
                pe.wait_ge(pl_ready, KP)
                for c in range(4):
                    w, a = unit(j + c)
                    wait(pe, acc_free[a], w)
                    ins = products(s, a, range(KP), lambda k: ph[:, k, :], lambda k: pl[:, k, :],
                                   True, True, lambda k: k * 4 * P + c * P)
                    ins.then_inc(unit_done if c == 3 else ple_done, 1)

            def row_factor(n):
                for r in range(RT):
                    size = P if r < RT - 1 else DEC
                    pe.wait_ge(diag_ready, RT * n + r + 1)
                    ins = nc.tensor.matmul(small[:, r * P:r * P + size], ones[0:size, :],
                                           diag[0:size, P * (r % 4):P * (r % 4) + size], start=True, stop=True)
                    ins.then_inc(bcast_done, 1)

            def row_sums(n):
                for r in range(RT):
                    ins = nc.tensor.matmul(ret_s[:, r:r + 1], sqacc[:, r * P:(r + 1) * P], ones[:, 0:1],
                                           start=True, stop=True)
                ins.then_inc(sums_done, 1)

            pe.wait_ge(tables_in, 32)
            pe.wait_ge(gains_in, 16 * 5)
            pe.wait_ge(init_done, 1)
            nc.tensor.transpose(small[:, 1536:1536 + 4 * KD], g_row[:, :], ident[0:4 * KD, 0:4 * KD])
            nc.tensor.matmul(small[:, 1600:1600 + HEADS], ones[0:1, :], sink_row[0:1, :],
                             start=True, stop=True).then_inc(gain_t, 1)
            pe.wait_ge(gain_ready, 1)
            for r in range(RT):
                pe.wait_ge(x_in[r], 16)
            for k in range(KD + KP):
                if k >= 2:
                    pe.wait_ge(xt_copied, k - 1)
                if k == KD:
                    pe.wait_ge(p_in, 32)
                at = 1024 * (k % 2)
                src, col = (x_row, k * P) if k < KD else (p_row, (k - KD) * P)
                for r in range(RT):
                    size = P if r < RT - 1 else DEC
                    ins = nc.tensor.transpose(small[:, at + r * P:at + r * P + size],
                                              src[0:size, r, col:col + P], ident[0:size, 0:size])
                ins.then_inc(xt_psum, 1)
            pe.wait_ge(xt_copied, KD + 1)
            row_factor(0)

            run_unit(unit(U_KV), unit(J_KV), (xh, xl), ready=lambda k: pe.wait_ge(xl_ready, k + 1))
            run_unit(unit(U_KV + 1), unit(J_KV + 1), (xh, xl))
            with pe.Fori(0, GROUP // 2) as i:
                for n in range(2):
                    run_unit(unit(U_Q + n, 2, i), unit(J_Q + n, 2, i), (xh, xl))
            pe.wait_ge(va_ready, 1)
            pe.wait_ge(rb_ready, 1)
            pe.wait_ge(kt_ready, 1)
            pe.wait_ge(cache_in, 32)
            vt_tmp = prob[:, 0:3, :].rearrange("p j n -> p (j n)")
            for r in range(RT):
                size = P if r < RT - 1 else DEC
                nc.tensor.transpose(att[0:size, r * P:(r + 1) * P], vt_tmp[:, r * P:r * P + size], ident)
            nc.tensor.transpose(small[:, 1024:1152], kt[:, P + SEQ - P:P + SEQ], ident)
            nc.tensor.transpose(small[0:DEC, 1152:1280], kt[:, P + SEQ:P + ROWS], ident)
            nc.tensor.transpose(small[:, 1536:1664], ck_row[:, :], ident).then_inc(kv_t, 1)

            def att_piece(piece, g, b):
                n = 2 * b + g
                if piece == "A":
                    if isinstance(b, int) and b == 0 and g == 0:
                        pe.wait_ge(va_rows, 2)
                    pe.wait_ge(att_staged, b + 1)
                    if isinstance(b, int) and b == RH:
                        pe.wait_ge(cache_staged, 1)
                    wait(pe, att_out, n)
                    wait(pe, v_rows, 2 * b)
                    for j in range(GROUP):
                        ins = nc.tensor.matmul(att[:, j * KW:(j + 1) * KW], q_st[64 * g:64 * g + 64, j, :],
                                               k_st[64 * g:64 * g + 64, :], start=True, stop=True)
                    ins.then_inc(att_score, 1)
                elif piece == "B":
                    pe.wait_ge(att_prob, n + 1)
                    pe.wait_ge(att_top, n + 1)
                    for t in range(2):
                        for j in range(GROUP):
                            ins = nc.tensor.transpose(att[:, t * 512 + j * P:t * 512 + (j + 1) * P],
                                                      prob[:, j, t * P:(t + 1) * P], ident)
                    ins.then_inc(att_t, 1)
                elif piece == "C":
                    pe.wait_ge(att_t0, n + 1)
                    pe.wait_ge(att_t1, n + 1)
                    for t in range(2):
                        ins = nc.tensor.matmul(att[64 * g:64 * g + 64, 0:512], v_st[:, t, 64 * g:64 * g + 64],
                                               prob_t[:, t, :], start=t == 0, stop=t == 1)
                    ins.then_inc(att_pv, 1)

            def ret_piece(piece, c, r, slot):
                n = 5 * r + c
                if piece == "A":
                    pe.wait_ge(ret_sd, n + CREDIT)
                    pe.wait_ge(ret_kd, n + CREDIT)
                    pe.wait_ge(ret_gated, 5 * r + max(0, c - 1) + CREDIT)
                    pe.wait_ge(rotated, 2 * r + 2)
                    pe.wait_ge(ret_kst, n + 1 + CREDIT)
                    pe.wait_ge(tables_in, 32)
                    nc.tensor.matmul(ret_s, rk_st[:, c % 2, :], qr[:, slot, c * P:(c + 1) * P] if isinstance(slot, int)
                                     else qr[:, bass.ds(slot, 1), c * P:(c + 1) * P].rearrange("p a n -> p (a n)"),
                                     start=True, stop=True)
                    nc.tensor.transpose(ret_kt, rk_st[:, c % 2, :], ident).then_inc(ret_A, 1)
                elif piece == "B":
                    pe.wait_ge(ret_sd, n + 1 + CREDIT)
                    pe.wait_ge(ret_kd, n + 1 + CREDIT)
                    pe.wait_ge(ret_qd, n + 1 + CREDIT)
                    pe.wait_ge(ret_state, n + CREDIT)
                    pe.wait_ge(ret_norm, n + CREDIT)
                    pe.wait_ge(v_rows, 2 * r + 2)
                    v = vr[:, slot, c, :] if isinstance(slot, int) else \
                        vr[:, bass.ds(slot, 1), c, :].rearrange("p a n -> p (a n)")
                    if c == RT - 1:
                        pe.wait_ge(state_in_s, 16 * (r + 1))
                    pe.wait_ge(tables_in, 32)
                    nc.tensor.matmul(ret_o, s_dec[:, c % 2, :], v, start=True, stop=c == 0)
                    if c > 0:
                        nc.tensor.matmul(ret_o, q_dec[:, c % 2, :], (state_s if c == RT - 1 else state_p)[:, :],
                                         start=False, stop=True)
                    nc.tensor.matmul(ret_dl, k_dec[:, c % 2, :], v, start=True, stop=True).then_inc(ret_B, 1)
                elif piece == "C":
                    pe.wait_ge(ret_norm, n + 1 + CREDIT)
                    pe.wait_ge(ret_gated, n + CREDIT)
                    pe.wait_ge(ret_sd, 5 * r + min(c + 2, RT) + CREDIT)
                    pe.wait_ge(ret_kd, 5 * r + min(c + 2, RT) + CREDIT)
                    for e in range(EV):
                        ins = nc.tensor.transpose(ret_ot[:, e * P:(e + 1) * P], o_norm[:, c % 2, e * P:(e + 1) * P], ident)
                    ins.then_inc(ret_C, 1)

            def v_transposes(e, h):
                w, a = unit(J_HEAD + (3, 4)[e], 6, h)
                pe.wait_ge(acc_free[a], w + 1)
                wait(pe, v_rows, 2 * h + e)
                pe.wait_ge(att_t1, 2 * h + 2)
                pe.wait_ge(att_out, 2 * h + 2)
                for r in range(RT - 1):
                    nc.tensor.transpose(att[:, r * P:(r + 1) * P], zt[:, a, r * P:(r + 1) * P], ident)
                nc.tensor.transpose(att[0:DEC, SEQ:SEQ + P], zt[:, a, SEQ:ROWS], ident).then_inc(v_t, 1)

            def pieces(place, h, b, r, slot):
                for kind, piece, c in PLACES[place]:
                    if kind == "att":
                        att_piece(piece, c, b)
                    elif kind == "ret" and r is not None:
                        ret_piece(piece, c, r, slot)
                    elif kind == "v" and h is not None:
                        v_transposes(c, h)

            def six_jobs(u, j, per, i, h, b, r, slot):
                for t in range(6):
                    run_unit(unit(u + t, per, i), unit(j + t, per, i), (xh, xl),
                             between=lambda: pieces(2 * t, h, b, r, slot))
                    pieces(2 * t + 1, h, b, r, slot)

            pe.wait_ge(ckt_ready, 1)
            pe.wait_ge(kv_rows, 1)
            six_jobs(U_HEAD, J_HEAD, 6, 0, 0, 0, None, None)
            with pe.Fori(1, RH) as h:
                six_jobs(U_HEAD, J_HEAD, 6, h, h, h, h - 1, (h - 1) % 2)
            six_jobs(U_GATE, J_GATE, 6, 0, None, RH, RH - 1, (RH - 1) % 2)
            for n in (6, 7):
                run_unit(unit(U_GATE + n), unit(J_GATE + n), (xh, xl))

            def merge(u, j, per, c, ready=None):
                run_unit(unit(u, per, c), unit(j, per, c), (ah, al), ks=GROUP, ready=ready and ready[0])
                run_unit(unit(u + 1, per, c), unit(j + 1, per, c), (rh, rl), ready=ready and ready[1])

            merge(U_MRG, J_MRG, 4, 0, ready=(lambda k: pe.wait_ge(branch_lo, k + 1),
                                             lambda k: pe.wait_ge(branch_lo, GROUP + k + 1)))
            for n in (2, 3):
                run_unit(unit(U_MRG + n), unit(J_MRG + n), (xh, xl))
            with pe.Fori(1, 4) as c:
                merge(U_MRG, J_MRG, 4, c)
                for n in (2, 3):
                    run_unit(unit(U_MRG + n, 4, c), unit(J_MRG + n, 4, c), (xh, xl))
            with pe.Fori(0, 4) as c:
                merge(U_MRG2, J_MRG2, 2, c)
            run_unit(unit(U_OUT), unit(J_OUT), (yh, ml), ready=lambda k: pe.wait_ge(m_lo, k + 1))
            run_unit(unit(U_OUT + 1), unit(J_OUT + 1), (yh, ml))
            with pe.Fori(1, KD // 2) as i:
                for n in range(2):
                    run_unit(unit(U_OUT + n, 2, i), unit(J_OUT + n, 2, i), (yh, ml))
            run_ple(U_P0, J_P0, 0)
            pe.wait_ge(sq_added, KD)
            row_sums(0)
            row_factor(1)
            for half, (uf, jf, ud, jd) in enumerate(((U_FA, J_FA, U_DA, J_DA), (U_FB, J_FB, U_DB, J_DB))):
                if half == 0:
                    run_unit(unit(uf), unit(jf), (yh, yl), ready=lambda k: pe.wait_ge(y_lo, k + 1))
                    pe.wait_ge(sq_added, 2 * KD)
                    row_sums(1)
                    run_unit(unit(uf + 1), unit(jf + 1), (yh, yl))
                    row_factor(2)
                else:
                    run_unit(unit(uf), unit(jf), (yh, yl))
                    run_unit(unit(uf + 1), unit(jf + 1), (yh, yl))
                with pe.Fori(1, FTH) as i:
                    run_unit(unit(uf, 2, i), unit(jf, 2, i), (yh, yl))
                    run_unit(unit(uf + 1, 2, i), unit(jf + 1, 2, i), (yh, yl))

                def down(c0, i, n, ready=None):
                    ja = unit(jd + n, 2, i)
                    run_unit(unit(ud + 2 * n, 4, i), ja, (fh, fl), ks=DOWN_K[0], last=False, ready=ready)
                    run_unit(unit(ud + 2 * n + 1, 4, i), ja, (fh, fl), ks=DOWN_K[1], k0=DOWN_K[0], first=False,
                             ready=ready)

                down(0, 0, 0, ready=lambda k: pe.wait_ge(f_lo, half * FTH + k + 1))
                down(0, 0, 1)
                with pe.Fori(1, KD // 2) as i:
                    down(0, i, 0)
                    down(0, i, 1)
            run_ple(U_P1, J_P1, 1)
            pe.wait_ge(sq_added, 3 * KD)
            row_sums(2)
            row_factor(3)

            def y_transposes(c, n):
                pe.wait_ge(y_ready, c + 1)
                wait(pe, y_rows, c - 1)
                at = 1024 * n
                for r in range(RT):
                    size = P if r < RT - 1 else DEC
                    ins = nc.tensor.transpose(small[0:size, at + r * P:at + (r + 1) * P],
                                              yt[:, n, r * P:r * P + size], ident)
                ins.then_inc(y_t, 1)

            run_unit(unit(U_PG), unit(J_PG), (yh, yl), ready=lambda k: pe.wait_ge(y_lo, KD + k + 1))
            run_unit(unit(U_PG + 1), unit(J_PG + 1), (yh, yl))
            y_transposes(0, 0)
            with pe.Fori(1, KD // 2) as i:
                run_unit(unit(U_PG, 2, i), unit(J_PG, 2, i), (yh, yl))
                y_transposes(2 * i - 1, 1)
                run_unit(unit(U_PG + 1, 2, i), unit(J_PG + 1, 2, i), (yh, yl))
                y_transposes(2 * i, 0)
            y_transposes(KD - 1, 1)

        @block.scalar
        def _(act):
            def split_hi(vs, n=KD * P):
                v, s = vs
                act.wait_ge(loaded[s], 32 * (v + 1))
                wait(act, unit_done, 2 * v + s - 1)
                nc.scalar.activation(whi[:, s, 0:n], raw[:, s, 0:n], ACT.Copy).then_inc(hi_ready, 1)

            def settled():
                act.sem_inc(act_passed, 1)

            act.dma_start(tab[:, :], table_in[:, 0:T_COLS]).then_inc(tables_in, 16)
            for n, g in enumerate((g_mix_pre, g_mix_post, g_ffn_pre, g_ffn_post)):
                act.dma_start(g_row[n * KD:(n + 1) * KD, :], g[0].rearrange("(k p) -> k p", p=P)).then_inc(gains_in, 16)
            act.dma_start(sink_row[:, :], sinks_in).then_inc(gains_in, 16)
            act.dma_start(rot[:, :, :], table_in[:, T_ROT:T_ALL].rearrange("p (a n) -> p a n", a=2)).then_inc(tables_in, 16)
            act.dma_start(p_row[:, 0:RT - 1, :], p_p[0, 0].rearrange("(r p) n -> p r n", p=P)).then_inc(p_in, 16)
            act.dma_start(p_row[0:DEC, RT - 1, :], p_s[0, 0]).then_inc(p_in, 16)
            for s_ in (state_p_out, state_s_out):
                act.sem_inc(s_, 16 * CREDIT)
            act.dma_start(ck_row[:, :], cache_k[0, 0].rearrange("n h d -> n (h d)")).then_inc(cache_in, 16)
            act.dma_start(cva[:, :], cache_v[0, 0].rearrange("n h d -> n (h d)")).then_inc(cache_in, 16)
            act.wait_ge(init_done, 1)
            for r in range(RT):
                size = P if r < RT - 1 else DEC
                act.wait_ge(x_in[r], 16)
                wait(act, squares_ready, r)
                nc.scalar.activation(square[0:size, :], x_row[0:size, r, :], ACT.Square,
                                     accum_out=rowsum[0:size, r:r + 1]).then_inc(squares_ready, 1)
            act.wait_ge(gain_ready, 1)
            for k in range(KD):
                act.wait_ge(xt_copied, k + 1)
                nc.scalar.activation(xh[:, k, :], x_t[:, k, :], ACT.Copy,
                                     scale=gains[:, k:k + 1]).then_inc(xh_ready, 1)
            split_hi(unit(0))
            split_hi(unit(1))
            for k in range(KP):
                act.wait_ge(xt_copied, KD + k + 1)
                nc.scalar.activation(ph[:, k, :], (ta, tb)[k][:, :], ACT.Copy).then_inc(ph_ready, 1)

            def row_factor(n):
                act.wait_ge(bcast_done, RT * (n + 1))
                nc.scalar.activation(rb[:, :], small[:, 0:ROWS], ACT.Copy).then_inc(rb_ready, 1)

            row_factor(0)
            for n in range(2):
                split_hi(unit(2 + n))
            with act.Fori(0, GROUP // 2) as i:
                for n in range(2):
                    split_hi(unit(U_Q + 2 + n, 2, i))
            act.wait_ge(kv_t, 1)
            nc.scalar.activation(va[0:DEC, RT, :], att[0:DEC, SEQ:SEQ + P], ACT.Copy).then_inc(va_rows, 1)
            nc.scalar.activation(k_row[:, 0, :], small[:, 1024:1152], ACT.Copy)
            nc.scalar.activation(k_row[0:DEC, 1, :], small[0:DEC, 1152:1280], ACT.Copy).then_inc(kv_rows, 1)

            def att_piece(piece, g, b):
                n = 2 * b + g
                if piece == "A":
                    act.wait_ge(att_top, n + 1)
                    for j in range(GROUP):
                        nc.scalar.activation(prob[:, j, :], prob[:, j, :], ACT.Exp, bias=neg_top[:, j:j + 1],
                                             accum_out=den[:, j:j + 1])
                    nc.scalar.activation(sink_exp[:, :], top[:, :], ACT.Exp).then_inc(att_exp, 1)
                elif piece == "B":
                    act.wait_ge(att_t, n + 1)
                    nc.scalar.activation(prob_t[:, 0, :], att[:, 0:512], ACT.Copy).then_inc(att_t0, 1)
                elif piece == "C":
                    act.wait_ge(att_pv, n + 1)
                    size = DEC if isinstance(b, int) and b == RH else P
                    src = att[64 * g:64 * g + 64, 0:512].rearrange("p (j n) -> p j n", j=GROUP)[:, :, 0:size]
                    settled()
                    nc.scalar.activation(o_att[64 * g:64 * g + 64, :, span(P * b, size)], src, ACT.Copy).then_inc(att_out, 1)

            def head_job(t, h):
                w, a = unit(J_HEAD + t, 6, h)
                if t in (0, 2):
                    act.wait_ge(acc_free[a], w + 1)
                    m = 2 * h + t // 2
                    wait(act, rotated, m)
                    wait(act, g_ready, m)
                    nc.scalar.activation(tb[0:64, :], zt[64:128, a, :], ACT.Copy)
                    nc.scalar.activation(tb[64:128, :], zt[0:64, a, :], ACT.Copy).then_inc(swap_ready, 1)
                elif t in (1, 5):
                    act.wait_ge(acc_free[a], w + 1)
                    m = 2 * h + t // 5
                    wait(act, g_ready, m)
                    act.wait_ge(rotated, m + 1)
                    nc.scalar.activation(tb[:, :], zt[:, a, :], ACT.Sigmoid).then_inc(sg_ready, 1)

            def state_piece(piece, c, r):
                if piece == "A" and c == 1:
                    act.wait_ge(state_s_out, 16 * (r + CREDIT))
                    settled()
                    act.dma_start(state_s[:, :], state_in[0, 0, span(r, 1)].rearrange("a d e -> d (a e)")
                                  ).then_inc(state_in_s, 16)
                elif piece == "B" and c >= RT - 2:
                    out, st, done = ((r_p, state_p, state_p_out), (r_s, state_s, state_s_out))[c - (RT - 2)]
                    act.wait_ge(ret_state, 5 * r + c + 1 + CREDIT)
                    settled()
                    act.dma_start(out[0, 0, span(r, 1)].rearrange("a d e -> d (a e)"), st[:, :]).then_inc(done, 16)

            def pieces(place, b, r):
                for kind, piece, c in PLACES[place]:
                    if kind == "att":
                        att_piece(piece, c, b)
                    elif kind == "ret" and r is not None:
                        state_piece(piece, c, r)

            def head(h, b, r):
                for t in range(6):
                    pieces(2 * t, b, r)
                    split_hi(unit(U_HEAD + t + 2, 6, h))
                    head_job(t, h)
                    pieces(2 * t + 1, b, r)

            head(0, 0, None)
            with act.Fori(1, RH) as h:
                head(h, h, h - 1)

            def gate(w, a, dst):
                act.wait_ge(acc_free[a], w + 1)
                settled()
                nc.scalar.activation(dst, zt[:, a, :], ACT.Sigmoid).then_inc(gate_sig[a], 1)

            for t in range(8):
                if t < 6:
                    pieces(2 * t, RH, RH - 1)
                    split_hi(unit(U_GATE + t + 2))
                else:
                    split_hi(unit(U_MRG + t - 6), n=(GROUP if t == 6 else KD) * P)
                w, a = unit(J_GATE + t)
                if t == 0:
                    act.wait_ge(x_saved, 16)
                gate(w, a, sig[:, t // 2, t % 2, :])
                if t < 6:
                    pieces(2 * t + 1, RH, RH - 1)
            act.wait_ge(att_pv, 2 * (RH + 1))
            act.wait_ge(att_out, 2 * (RH + 1))
            act.wait_ge(ret_C, 5 * RH + CREDIT)
            act.wait_ge(ret_gated, 5 * RH + CREDIT)
            act.wait_ge(state_p_out, 16 * (RH + CREDIT))
            act.wait_ge(state_s_out, 16 * (RH + CREDIT))
            act.wait_ge(out_done, 16 * 6)
            for k in range(GROUP + KD):
                dst, src = (ah[:, k, :], o_att[:, k, :]) if k < GROUP else (rh[:, k - GROUP, :], o_ret[:, k - GROUP, :])
                nc.scalar.activation(dst, src, ACT.Copy).then_inc(branch_hi, 1)

            def merged(c):
                act.wait_ge(m_ready, c + 1)
                settled()
                nc.scalar.activation(yh[:, span(c, 1), :].rearrange("p a n -> p (a n)"), ta[:, :], ACT.Copy).then_inc(m_hi, 1)

            with act.Fori(0, 4) as c:
                for n in range(4):
                    nxt = (2, 3, 4, 5)[n]
                    split_hi(unit(U_MRG + nxt, 4, c), n=(GROUP if n == 2 else KD) * P)
                    if n == 1:
                        merged(c)
                    if n >= 2:
                        w, a = unit(J_MRG + n, 4, c)
                        act.wait_ge(m_ready, c + 1)
                        gate(w, a, sig[:, span(c, 1), n - 2, :].rearrange("p a n -> p (a n)"))
            with act.Fori(0, 3) as c:
                split_hi(unit(U_MRG2 + 2, 2, c), n=GROUP * P)
                split_hi(unit(U_MRG2 + 3, 2, c))
                merged(c + 4)
            split_hi(unit(U_OUT))
            split_hi(unit(U_OUT + 1))
            merged(7)

            def store_square(i, n):
                split_hi(unit(U_OUT + 2 + n, 2, i))
                w, a = unit(J_OUT + n, 2, i)
                act.wait_ge(unit_done, U_OUT + n + 1 + 2 * i)
                settled()
                nc.scalar.activation(halves(wide[:, span(2 * i + n, 1), :].rearrange("p a n -> p (a n)")), acc_of(a),
                                     ACT.Copy)
                wait(act, sq_added, 2 * i + n)
                nc.scalar.activation(halves(tb[:, :]), acc_of(a), ACT.Square).then_inc(acc_free[a], 1)

            store_square(0, 0)
            store_square(0, 1)
            with act.Fori(1, KD // 2) as i:
                store_square(i, 0)
                store_square(i, 1)
            split_hi(unit(U_FA + 1))

            def split_res(m, gain):
                with act.Fori(0, KD // 2) as i:
                    for n in range(2):
                        k = 2 * i + n
                        act.wait_ge(res_ready, KD * m + k + 1)
                        settled()
                        dst = yh[:, span(k, 1), :].rearrange("p a n -> p (a n)")
                        src = res[:, span(k, 1), :].rearrange("p a n -> p (a n)")
                        if gain is None:
                            nc.scalar.activation(dst, src, ACT.Copy).then_inc(y_hi, 1)
                        else:
                            nc.scalar.activation(dst, src, ACT.Copy, scale=gains[:, span(gain + k, 1)]).then_inc(y_hi, 1)
                            act.wait_ge(sq_added, KD + k - 1)
                            settled()
                            nc.scalar.activation((ta, tb)[n][:, :], src, ACT.Square).then_inc(sq_ready, 1)

            row_factor(1)
            split_res(0, 2 * KD)
            act.wait_ge(sq_added, 2 * KD)
            row_factor(2)
            for half, (uf, jf, ud, jd) in enumerate(((U_FA, J_FA, U_DA, J_DA), (U_FB, J_FB, U_DB, J_DB))):
                def ffn(i, ahead):
                    split_hi(*ahead[0])
                    act.wait_ge(acc_free[jf % 2], unit(jf, 2, i)[0] + 1)
                    nc.scalar.activation(tb[:, :], zt[:, jf % 2, :], ACT.Sigmoid).then_inc(silu_sg, 1)
                    split_hi(*ahead[1])
                    act.wait_ge(f_ready, half * FTH + i + 1)
                    settled()
                    nc.scalar.activation(fh[:, span(i, 1), :].rearrange("p a n -> p (a n)"), ta[:, :], ACT.Copy).then_inc(f_hi, 1)

                with act.Fori(0, FTH - 1) as i:
                    ffn(i, ((unit(uf + 2, 2, i),), (unit(uf + 3, 2, i),)))
                ffn(FTH - 1, ((unit(ud), DOWN_K[0] * P), (unit(ud + 1), DOWN_K[1] * P)))

                def down(i, n, last):
                    size = (KD * P, KD * P) if last else (DOWN_K[0] * P, DOWN_K[1] * P)
                    for m in range(2):
                        split_hi(unit(ud + 2 * n + 2 + m, 4, i), n=size[m])
                    if half == 1:
                        w, a = unit(jd + n, 2, i)
                        c = 2 * i + n
                        act.wait_ge(acc_free[a], w + 1)
                        act.wait_ge(sq_added, 2 * KD + c)
                        settled()
                        nc.scalar.activation(tb[:, :], wide[:, span(c, 1), :].rearrange("p a n -> p (a n)"),
                                             ACT.Square).then_inc(sq_ready, 1)

                with act.Fori(0, KD // 2 - 1) as i:
                    down(i, 0, False)
                    down(i, 1, False)
                down(KD // 2 - 1, 0, False)
                down(KD // 2 - 1, 1, True)
            split_hi(unit(U_PG + 1))
            row_factor(3)
            split_res(1, None)

            def y_piece(i, n, ahead):
                w, a = unit(J_PG + n, 2, i)
                c = 2 * i + n
                if ahead:
                    split_hi(unit(U_PG + 2 + n, 2, i))
                act.wait_ge(unit_done, U_PG + 1 + c)
                wait(act, y_ready, c)
                nc.scalar.activation(halves(tb[:, :]), acc_of(a), ACT.Sigmoid).then_inc(acc_free[a], 1)

            y_piece(0, 0, True)
            y_piece(0, 1, True)
            with act.Fori(1, KD // 2 - 1) as i:
                y_piece(i, 0, True)
                y_piece(i, 1, True)
            y_piece(KD // 2 - 1, 0, False)
            y_piece(KD // 2 - 1, 1, False)

        @block.vector
        def _(dve):
            def settled():
                dve.sem_inc(dve_passed, 1)

            def split_lo(vs, n=KD * P):
                v, s = vs
                dve.wait_ge(hi_ready, 2 * v + s + 1)
                nc.vector.tensor_tensor(wlo[:, s, 0:n], raw[:, s, 0:n], whi[:, s, 0:n].bitcast(F32),
                                        ALU.subtract).then_inc(lo_ready, 1)

            def row_factor(n, src, done):
                dve.wait_ge(done[0], done[1])
                nc.vector.tensor_scalar(rowvar[:, 0:RT], src, 1.0 / D, EPS, ALU.mult, ALU.add).then_inc(var_ready, 1)
                dve.wait_ge(rstd_ready, n + 1)
                for r in range(RT):
                    if r == 4:
                        dve.wait_ge(bcast_done, RT * n + 1)
                    nc.vector.tensor_scalar(diag[:, P * (r % 4):P * (r % 4) + P], ident, rstd[:, r:r + 1], None,
                                            ALU.mult).then_inc(diag_ready, 1)

            nc.vector.memset(ones[:, :], 1.0)
            nc.vector.memset(neg_half[:, :], -0.5)
            nc.vector.memset(rowsum[:, :], 0.0).then_inc(init_done, 1)
            dve.wait_ge(gain_t, 1)
            nc.vector.tensor_copy(gains[:, :], small[:, 1536:1536 + 4 * KD])
            nc.vector.tensor_copy(sinks[:, :], small[:, 1600:1600 + HEADS]).then_inc(gain_ready, 1)
            dve.wait_ge(gain_ready, 1)
            for k in range(KD):
                dve.wait_ge(xt_psum, k + 1)
                nc.vector.tensor_copy(x_t[:, k, :], small[:, 1024 * (k % 2):1024 * (k % 2) + ROWS]).then_inc(xt_copied, 1)
                dve.wait_ge(xt_copied, k + 1)
                dve.wait_ge(xh_ready, k + 1)
                nc.vector.scalar_tensor_tensor(xl[:, k, :], x_t[:, k, :], gains[:, k:k + 1], xh[:, k, :].bitcast(F32),
                                               ALU.mult, ALU.subtract).then_inc(xl_ready, 1)
            for k in range(KP):
                dve.wait_ge(xt_psum, KD + k + 1)
                nc.vector.tensor_copy((ta, tb)[k][:, :], small[:, 1024 * (k % 2):1024 * (k % 2) + ROWS]).then_inc(xt_copied, 1)
            split_lo(unit(0))
            split_lo(unit(1))
            for k in range(KP):
                dve.wait_ge(ph_ready, k + 1)
                nc.vector.tensor_tensor(pl[:, k, :], (ta, tb)[k][:, :], ph[:, k, :].bitcast(F32),
                                        ALU.subtract).then_inc(pl_ready, 1)
            dve.wait_ge(pl_ready, KP)
            row_factor(0, rowsum[:, 0:RT], (squares_ready, RT))

            def scaled_out(dst, w, a, u):
                dve.wait_ge(unit_done, u + 1)
                nc.vector.tensor_tensor(halves(dst), acc_of(a), halves(rb[:, :]), ALU.mult).then_inc(acc_free[a], 1)

            dve.wait_ge(rb_ready, 1)
            for n in range(2):
                split_lo(unit(2 + n))
                dve.wait_ge(unit_done, n + 1)
                if n == 1:
                    vt_tmp = prob[:, 0:3, :].rearrange("p j n -> p (j n)")[:, 0:ROWS]
                nc.vector.tensor_tensor(halves(kt[:, P:P + ROWS] if n == 0 else vt_tmp), acc_of(n), halves(rb[:, :]),
                                        ALU.mult).then_inc(acc_free[n], 1)
            dve.wait_ge(acc_free[1], 1)
            dve.wait_ge(acc_free[0], 1)
            nc.vector.memset(kt[:, P + ROWS:P + PADROWS], 0.0)
            nc.vector.memset(kt[:, 0:P], 0.0).then_inc(kt_ready, 1)
            nc.vector.memset(va[:, 0, :], 0.0)
            nc.vector.memset(va[64:128, RT, :], 0.0).then_inc(va_ready, 1)
            nc.vector.memset(qt[:, :, ROWS:PADROWS], 0.0)
            nc.vector.memset(qr[:, :, ROWS:PADROWS], 0.0)
            nc.vector.memset(kr[:, :, ROWS:PADROWS], 0.0)
            nc.vector.memset(vr[64:128, :, RT - 1, :], 0.0).then_inc(init_done, 1)
            with dve.Fori(0, GROUP // 2) as i:
                for n in range(2):
                    split_lo(unit(U_Q + 2 + n, 2, i))
                    w, a = unit(J_Q + n, 2, i)
                    scaled_out(qt[:, bass.ds(2 * i + n, 1), 0:ROWS].rearrange("p a n -> p (a n)"), w, a, U_Q + n + 2 * i)
            dve.wait_ge(kv_t, 1)
            nc.vector.tensor_copy(va[:, 1:RT, :], att[:, 0:512].rearrange("p (r n) -> p r n", n=P)).then_inc(va_rows, 1)
            nc.vector.tensor_copy(ckt[:, :], small[:, 1536:1664]).then_inc(ckt_ready, 1)

            def att_piece(piece, g, b):
                n = 2 * b + g
                if piece == "A":
                    dve.wait_ge(att_score, n + 1)
                    settled()
                    mask = 0 if isinstance(b, int) and b == 0 else (2 if isinstance(b, int) and b == RH else 1)
                    mcol = tab[:, T_MASK + mask * KW:T_MASK + (mask + 1) * KW]
                    for j in range(GROUP):
                        nc.vector.tensor_tensor_reduce(
                            out=prob[:, j, :], in0=att[:, j * KW:(j + 1) * KW], in1=mcol, scale=SCALE,
                            scalar=sinks[:, GROUP * g + j:GROUP * g + j + 1], op0=ALU.add, op1=ALU.max,
                            accum_out=top[:, j:j + 1]).then_inc(dve_top, 1)
                    dve.wait_ge(dve_top, 6 * n + 4)
                    nc.vector.tensor_scalar(neg_top[:, :], top[:, :], -1.0, None, ALU.mult).then_inc(dve_top, 1)
                    dve.wait_ge(dve_top, 6 * n + 5)
                    nc.vector.tensor_tensor(top[:, :], sinks[:, GROUP * g:GROUP * (g + 1)], neg_top[:, :],
                                            ALU.add).then_inc(att_top, 1)
                elif piece == "N":
                    dve.wait_ge(att_exp, n + 1)
                    nc.vector.tensor_tensor(den[:, :], den[:, :], sink_exp[:, :], ALU.add).then_inc(dve_top, 1)
                    dve.wait_ge(dve_top, 6 * n + 6)
                    nc.vector.reciprocal(den[:, :], den[:, :]).then_inc(att_den, 1)
                    dve.wait_ge(att_den, n + 1)
                    for j in range(GROUP):
                        ins = nc.vector.tensor_scalar(prob[:, j, :], prob[:, j, :], den[:, j:j + 1], None, ALU.mult)
                    ins.then_inc(att_prob, 1)
                elif piece == "B":
                    dve.wait_ge(att_t, n + 1)
                    nc.vector.tensor_copy(prob_t[:, 1, :], att[:, 512:1024]).then_inc(att_t1, 1)

            def row_tile(c):
                return (c * P, P if c < RT - 1 else DEC)

            def ret_piece(piece, c, r, slot):
                n = 5 * r + c
                at, size = row_tile(c)
                if piece == "A":
                    dve.wait_ge(ret_B, n + 1 + CREDIT - earlier_use(c))
                    q = qr[:, span(slot, 1), c * P:(c + 1) * P].rearrange("p a n -> p (a n)")
                    nc.vector.tensor_tensor(q_dec[:, c % 2, :], q, tab[:, span(T_QD + P * r, P)], ALU.mult).then_inc(ret_qd, 1)
                    dve.wait_ge(ret_A, n + 1 + CREDIT)
                    nc.vector.tensor_tensor(s_dec[:, c % 2, :], ret_s, tab[:, span(T_DEC + P * r, P)], ALU.mult).then_inc(ret_sd, 1)
                    nc.vector.tensor_scalar(k_dec[:, c % 2, :], ret_kt, tab[:, span((T_KDS if c == RT - 1 else T_KD) + r, 1)],
                                            None, ALU.mult).then_inc(ret_kd, 1)
                elif piece == "B":
                    dve.wait_ge(ret_B, n + 1 + CREDIT)
                    if c == 0:
                        dve.wait_ge(state_p_out, 16 * (r + CREDIT))
                        nc.vector.tensor_scalar(state_p[:, :], ret_dl, 1.0, None, ALU.mult).then_inc(ret_state, 1)
                    else:
                        st, gl = (state_s, T_GLS) if c == RT - 1 else (state_p, T_GL)
                        nc.vector.scalar_tensor_tensor(st[:, :], st[:, :], tab[:, span(gl + r, 1)], ret_dl,
                                                       ALU.mult, ALU.add).then_inc(ret_state, 1)
                    nc.vector.bn_stats(stats[:, 0:6], ret_o).then_inc(dve_ret, 1)
                    dve.wait_ge(dve_ret, 2 * n + 1)
                    settled()
                    nc.vector.bn_aggr(moments[:, :], stats[:, 0:6]).then_inc(dve_ret, 1)
                    dve.wait_ge(dve_ret, 2 * n + 2)
                    nc.vector.tensor_scalar(grstd[:, :], moments[:, 1:2], GN_EPS, None, ALU.add).then_inc(ret_mom, 1)
                elif piece == "N":
                    dve.wait_ge(ret_grstd, n + 1 + CREDIT)
                    dve.wait_ge(ret_C, n + 1 + CREDIT - earlier_use(c))
                    nc.vector.tensor_scalar(o_norm[:, c % 2, :], ret_o, moments[:, 0:1], grstd[:, 0:1],
                                            ALU.subtract, ALU.mult).then_inc(ret_norm, 1)
                elif piece == "C":
                    dve.wait_ge(ret_C, n + 1 + CREDIT)
                    dve.wait_ge(g_ready, 2 * r + 2)
                    dst = o_ret[:, span(EV * r, EV), at:at + size]
                    src = ret_ot.rearrange("p (e n) -> p e n", e=EV)[:, :, 0:size]
                    gate = gr[:, span(slot, 1), :, at:at + size].rearrange("p a e n -> p (a e) n")
                    nc.vector.tensor_tensor(dst, src, gate, ALU.mult).then_inc(ret_gated, 1)

            def job_out(t, h):
                w, a = unit(J_HEAD + t, 6, h)
                if t in (1, 3):
                    wait(dve, g_ready, 2 * h + t // 3)
                scaled_out(zt[:, a, :], w, a, U_HEAD + t + 6 * h)

            def rotate(t, h, slot):
                m = 2 * h + t // 2
                dve.wait_ge(swap_ready, m + 1)
                nc.vector.tensor_tensor(tb[:, :], tb[:, :], rot[:, 1, :], ALU.mult).then_inc(dve_rot, 1)
                dve.wait_ge(dve_rot, m + 1)
                dve.wait_ge(cos_ready, m + 1)
                if not isinstance(h, int):
                    dve.wait_ge(ret_A, 5 * (h - 1) + CREDIT)
                    dve.wait_ge(ret_kst, 5 * (h - 1) + CREDIT)
                dst = (qr if t == 0 else kr)[:, span(slot, 1), 0:ROWS].rearrange("p a n -> p (a n)")
                nc.vector.tensor_tensor(dst, ta[:, :], tb[:, :], ALU.add).then_inc(rotated, 1)

            def v_out(e, h, slot):
                dve.wait_ge(v_t, 2 * h + e + 1)
                if not isinstance(h, int):
                    dve.wait_ge(ret_B, 5 * (h - 1) + CREDIT)
                dst = vr[:, span(slot, 1), :, e * P:(e + 1) * P].rearrange("p a r n -> p (a r) n")
                nc.vector.tensor_scalar(dst[:, 0:RT - 1, :], att[:, 0:512].rearrange("p (r n) -> p r n", n=P), 1.0, None,
                                        ALU.mult)
                nc.vector.tensor_scalar(dst[0:DEC, RT - 1, :], att[0:DEC, SEQ:SEQ + P], 1.0, None,
                                        ALU.mult).then_inc(v_rows, 1)

            def pieces(place, h, b, r, slot, rslot):
                for kind, piece, c in PLACES[place]:
                    if kind == "att":
                        att_piece(piece, c, b)
                    elif kind == "ret" and r is not None:
                        ret_piece(piece, c, r, rslot)
                    elif kind == "v" and h is not None:
                        v_out(c, h, slot)

            def head(h, b, r, slot, rslot):
                for t in range(6):
                    pieces(2 * t, h, b, r, slot, rslot)
                    job_out(t, h)
                    pieces(2 * t + 1, h, b, r, slot, rslot)
                    split_lo(unit(U_HEAD + t + 2, 6, h))
                    if t in (0, 2):
                        rotate(t, h, slot)

            head(0, 0, None, 0, None)
            with dve.Fori(1, RH) as h:
                head(h, h, h - 1, h % 2, (h - 1) % 2)

            for t in range(8):
                if t < 6:
                    pieces(2 * t, None, RH, RH - 1, None, (RH - 1) % 2)
                w, a = unit(J_GATE + t)
                if t == 1:
                    dve.wait_ge(g_ready, 2 * RH)
                wait(dve, gate_sig[a], t // 2)
                scaled_out(zt[:, a, :], w, a, U_GATE + t)
                if t < 6:
                    pieces(2 * t + 1, None, RH, RH - 1, None, (RH - 1) % 2)
                split_lo(unit(U_GATE + t + 2) if t < 6 else unit(U_MRG + t - 6), n=(GROUP if t == 6 else KD) * P)
            for k in range(GROUP + KD):
                dst, hi, src = (al[:, k, :], ah[:, k, :], o_att[:, k, :]) if k < GROUP else \
                    (rl[:, k - GROUP, :], rh[:, k - GROUP, :], o_ret[:, k - GROUP, :])
                dve.wait_ge(branch_hi, k + 1)
                nc.vector.tensor_tensor(dst, src, hi.bitcast(F32), ALU.subtract).then_inc(branch_lo, 1)

            def gated(u, j, per, c, n, slot, col):
                w, a = unit(j + n, per, c)
                dve.wait_ge(unit_done, u + n + 1 + per * c)
                dve.wait_ge(gate_sig[n], col + 1)
                gate = sig[:, span(slot, 1), n, :].rearrange("p a (h n) -> p (a h) n", h=2)
                nc.vector.tensor_tensor(halves((tb, mb)[n][:, :]), acc_of(a), gate, ALU.mult).then_inc(acc_free[a], 1)

            def merge_sum(c, w1, a1):
                dve.wait_ge(acc_free[a1], w1 + 1)
                wait(dve, m_lo, c)
                nc.vector.tensor_tensor(ta[:, :], tb[:, :], mb[:, :], ALU.add).then_inc(m_ready, 1)

            def merged_lo(c):
                dve.wait_ge(m_hi, c + 1)
                dst = ml[:, span(c, 1), :].rearrange("p a n -> p (a n)")
                hi = yh[:, span(c, 1), :].bitcast(F32).rearrange("p a n -> p (a n)")
                nc.vector.tensor_tensor(dst, ta[:, :], hi, ALU.subtract).then_inc(m_lo, 1)

            def merge_first(c):
                for n in range(4):
                    split_lo(unit(U_MRG + n + 2, 4, c), n=(GROUP if n == 2 else KD) * P)
                    if n < 2:
                        gated(U_MRG, J_MRG, 4, c, n, c, c)
                        if n == 1:
                            w1, a1 = unit(J_MRG + 1, 4, c)
                            merge_sum(c, w1, a1)
                    else:
                        if n == 2:
                            merged_lo(c)
                        w, a = unit(J_MRG + n, 4, c)
                        dve.wait_ge(gate_sig[a], 4 + c)
                        scaled_out(zt[:, a, :], w, a, U_MRG + n + 4 * c)

            dve.wait_ge(branch_lo, GROUP + KD)
            merge_first(0)
            with dve.Fori(1, 4) as c:
                merge_first(c)

            def merge_second(c, last):
                split_lo(unit(U_MRG2 + 2, 2, c), n=(KD if last else GROUP) * P)
                gated(U_MRG2, J_MRG2, 2, c, 0, c, c + 4)
                split_lo(unit(U_MRG2 + 3, 2, c))
                gated(U_MRG2, J_MRG2, 2, c, 1, c, c + 4)
                w1, a1 = unit(J_MRG2 + 1, 2, c)
                merge_sum(c + 4, w1, a1)
                merged_lo(c + 4)

            with dve.Fori(0, 3) as c:
                merge_second(c, False)
            merge_second(3, True)
            with dve.Fori(0, KD // 2) as i:
                for n in range(2):
                    split_lo(unit(U_OUT + 2 + n, 2, i))

            def proj_out(u, j, n):
                for c in range(4):
                    w, a = unit(j + c)
                    if c < 3:
                        dve.wait_ge(ple_done, 3 * n + c + 1)
                    else:
                        dve.wait_ge(unit_done, u + 1)
                    nc.vector.tensor_copy(halves(proj[:, 4 * n + c, :]), acc_of(a)).then_inc(acc_free[a], 1)

            proj_out(U_P0, J_P0, 0)
            split_lo(unit(U_FA + 1))
            row_factor(1, ret_s[:, 0:RT], (sums_done, 1))

            def new_res(m, k, gain):
                dve.wait_ge(scaled, KD * m + k + 1)
                if m == 0:
                    dve.wait_ge(x_back, 16)
                src = wide[:, span(k, 1), :].rearrange("p a n -> p (a n)")
                dst = res[:, span(k, 1), :].rearrange("p a n -> p (a n)")
                nc.vector.scalar_tensor_tensor(dst, src, gains[:, span(gain + k, 1)], dst, ALU.mult,
                                               ALU.add).then_inc(res_ready, 1)

            def res_lo(m, k, gain):
                dve.wait_ge(y_hi, KD * m + k + 1)
                src = res[:, span(k, 1), :].rearrange("p a n -> p (a n)")
                hi = yh[:, span(k, 1), :].bitcast(F32).rearrange("p a n -> p (a n)")
                dst = yl[:, span(k, 1), :].rearrange("p a n -> p (a n)")
                if gain is None:
                    nc.vector.tensor_tensor(dst, src, hi, ALU.subtract).then_inc(y_lo, 1)
                else:
                    nc.vector.scalar_tensor_tensor(dst, src, gains[:, span(gain + k, 1)], hi, ALU.mult,
                                                   ALU.subtract).then_inc(y_lo, 1)

            def residual(m, g_post, g_next):
                new_res(m, 0, g_post)
                with dve.Fori(1, KD) as k:
                    new_res(m, k, g_post)
                    res_lo(m, k - 1, g_next)
                res_lo(m, KD - 1, g_next)

            residual(0, KD, 2 * KD)
            row_factor(2, ret_s[:, 0:RT], (sums_done, 2))
            for half, (uf, jf, ud, jd) in enumerate(((U_FA, J_FA, U_DA, J_DA), (U_FB, J_FB, U_DB, J_DB))):
                def ffn(i, ahead):
                    split_lo(*ahead[0])
                    w, a = unit(jf, 2, i)
                    dve.wait_ge(rb_ready, 3)
                    scaled_out(zt[:, a, :], w, a, uf + 2 * i)
                    split_lo(*ahead[1])
                    w, a = unit(jf + 1, 2, i)
                    scaled_out(zt[:, a, :], w, a, uf + 1 + 2 * i)
                    dve.wait_ge(silu_ready, half * FTH + i + 1)
                    dve.wait_ge(acc_free[a], w + 1)
                    nc.vector.tensor_tensor(ta[:, :], ta[:, :], zt[:, a, :], ALU.mult).then_inc(f_ready, 1)
                    dve.wait_ge(f_hi, half * FTH + i + 1)
                    dst = fl[:, span(i, 1), :].rearrange("p a n -> p (a n)")
                    hi = fh[:, span(i, 1), :].bitcast(F32).rearrange("p a n -> p (a n)")
                    nc.vector.tensor_tensor(dst, ta[:, :], hi, ALU.subtract).then_inc(f_lo, 1)

                with dve.Fori(0, FTH - 1) as i:
                    ffn(i, ((unit(uf + 2, 2, i),), (unit(uf + 3, 2, i),)))
                ffn(FTH - 1, ((unit(ud), DOWN_K[0] * P), (unit(ud + 1), DOWN_K[1] * P)))

                def down(i, n, last):
                    size = (KD * P, KD * P) if last else (DOWN_K[0] * P, DOWN_K[1] * P)
                    for m in range(2):
                        split_lo(unit(ud + 2 * n + 2 + m, 4, i), n=size[m])
                    w, a = unit(jd + n, 2, i)
                    c = 2 * i + n
                    dve.wait_ge(unit_done, ud + 2 + 2 * c)
                    dst = wide[:, span(c, 1), :].rearrange("p a (h n) -> p (a h) n", h=2)
                    if half == 0:
                        nc.vector.tensor_scalar(dst, acc_of(a), 1.0, None, ALU.mult).then_inc(acc_free[a], 1)
                    else:
                        nc.vector.tensor_tensor(dst, acc_of(a), dst, ALU.add).then_inc(acc_free[a], 1)

                with dve.Fori(0, KD // 2 - 1) as i:
                    down(i, 0, False)
                    down(i, 1, False)
                down(KD // 2 - 1, 0, False)
                down(KD // 2 - 1, 1, True)
            proj_out(U_P1, J_P1, 1)
            split_lo(unit(U_PG + 1))
            row_factor(3, ret_s[:, 0:RT], (sums_done, 3))
            residual(1, 3 * KD, None)

            def y_piece(i, n, ahead):
                w, a = unit(J_PG + n, 2, i)
                c = 2 * i + n
                if ahead:
                    split_lo(unit(U_PG + 2 + n, 2, i))
                dve.wait_ge(acc_free[a], w + 1)
                wait(dve, y_t, c - 1)
                nc.vector.tensor_tensor(yt[:, n, :], tb[:, :], proj[:, span(c, 1), :].rearrange("p a n -> p (a n)"),
                                        ALU.mult).then_inc(dve_y, 1)
                dve.wait_ge(dve_y, c + 1)
                nc.vector.tensor_tensor(yt[:, n, :], yt[:, n, :], res[:, span(c, 1), :].rearrange("p a n -> p (a n)"),
                                        ALU.add).then_inc(y_ready, 1)

            def y_rows_out(c, n):
                dve.wait_ge(y_t, c + 1)
                wait(dve, y_out[n], 32 * (c // 2))
                nc.vector.tensor_scalar(y_row[:, n, 0:RT - 1, :],
                                        small[:, 1024 * n:1024 * n + 512].rearrange("p (r n) -> p r n", n=P),
                                        1.0, None, ALU.mult)
                nc.vector.tensor_scalar(y_row[0:DEC, n, RT - 1, :], small[0:DEC, 1024 * n + SEQ:1024 * n + SEQ + P],
                                        1.0, None, ALU.mult).then_inc(y_rows, 1)

            for c in range(KD):
                y_piece(c // 2, c % 2, c < KD - 2)
                if c >= 1:
                    y_rows_out(c - 1, (c - 1) % 2)
            y_rows_out(KD - 1, (KD - 1) % 2)

        @block.gpsimd
        def _(pool):
            def settled():
                pool.sem_inc(pool_passed, 1)

            for s_ in (ret_kst, ret_qd, ret_A, ret_sd, ret_kd, ret_B, ret_state, ret_grstd, ret_norm, ret_C, ret_gated):
                pool.sem_inc(s_, CREDIT)

            def power(n):
                pool.wait_ge(var_ready, n + 1)
                nc.gpsimd.tensor_tensor(rstd[:, 0:RT], rowvar[:, 0:RT], neg_half[:, 0:RT], ALU.pow).then_inc(rstd_ready, 1)

            power(0)
            pool.wait_ge(xt_copied, KD)
            pool.dma_start(scratch, x_t[:, :, :].rearrange("p k n -> p (k n)")).then_inc(x_saved, 16)
            half_rows = lambda ap: ap[0, 0].rearrange("n h d -> n (h d)")
            pool.wait_ge(kv_rows, 1)
            pool.wait_ge(va_rows, 2)
            pool.dma_start(half_rows(k_p), k_row[:, 0, :]).then_inc(out_done, 16)
            pool.dma_start(half_rows(v_p), va[:, RT - 1, :]).then_inc(out_done, 16)
            pool.dma_start(half_rows(k_s)[DEC:P, :], k_row[0:DEC, 1, :]).then_inc(out_done, 16)
            pool.dma_start(half_rows(v_s)[DEC:P, :], va[0:DEC, RT, :]).then_inc(out_done, 16)
            pool.dma_start(half_rows(k_s)[0:DEC, :], half_rows(cache_k)[DEC:P, :]).then_inc(out_done, 16)
            pool.dma_start(half_rows(v_s)[0:DEC, :], half_rows(cache_v)[DEC:P, :]).then_inc(out_done, 16)

            def stage_block(b):
                if isinstance(b, int) and b == 0:
                    pool.wait_ge(kt_ready, 1)
                    nc.gpsimd.tensor_copy(k_st[:, :], kt[:, 0:KW])
                    nc.gpsimd.tensor_copy(v_st[:, :, :], va[:, 0:2, :])
                    pool.wait_ge(init_done, 2)
                    pool.wait_ge(acc_free[0], J_HEAD // 2)
                    pool.wait_ge(acc_free[1], J_HEAD // 2)
                    nc.gpsimd.tensor_copy(q_st[:, :, :], qt[:, :, 0:P]).then_inc(att_staged, 1)
                else:
                    pool.wait_ge(att_pv, 2 * b)
                    settled()
                    nc.gpsimd.tensor_copy(k_st[:, :], kt[:, span(P * b, KW)])
                    nc.gpsimd.tensor_copy(v_st[:, :, :], va[:, span(b, 2), :])
                    nc.gpsimd.tensor_copy(q_st[:, :, :], qt[:, :, span(P * b, P)]).then_inc(att_staged, 1)

            def stage_k(c, r, slot):
                pool.wait_ge(ret_A, 5 * r + max(0, c - 1) + CREDIT)
                pool.wait_ge(rotated, 2 * r + 2)
                settled()
                nc.gpsimd.tensor_copy(rk_st[:, c % 2, :], kr[:, span(slot, 1), c * P:(c + 1) * P].rearrange(
                    "p a n -> p (a n)")).then_inc(ret_kst, 1)

            def ret_piece(piece, c, r, slot):
                n = 5 * r + c
                if piece == "A" and c < RT - 1:
                    stage_k(c + 1, r, slot)
                elif piece == "B":
                    pool.wait_ge(ret_mom, n + 1)
                    nc.gpsimd.tensor_tensor(grstd[:, :], grstd[:, :], neg_half[:, 0:1], ALU.pow).then_inc(ret_grstd, 1)

            def head_job(t, h, slot):
                w, a = unit(J_HEAD + t, 6, h)
                if t in (0, 2):
                    m = 2 * h + t // 2
                    pool.wait_ge(acc_free[a], w + 1)
                    wait(pool, rotated, m)
                    nc.gpsimd.tensor_tensor(ta[:, :], zt[:, a, :], rot[:, 0, :], ALU.mult).then_inc(cos_ready, 1)
                elif t in (1, 5):
                    m = 2 * h + t // 5
                    pool.wait_ge(sg_ready, m + 1)
                    if not isinstance(h, int):
                        pool.wait_ge(ret_gated, 5 * (h - 1) + CREDIT)
                    settled()
                    nc.gpsimd.tensor_tensor(gr[:, span(slot, 1), t // 5, :].rearrange("p a n -> p (a n)"),
                                            zt[:, a, :], tb[:, :], ALU.mult).then_inc(g_ready, 1)

            def pieces(place, r, rslot):
                for kind, piece, c in PLACES[place]:
                    if kind == "ret" and r is not None:
                        ret_piece(piece, c, r, rslot)

            def head(h, r, slot, rslot):
                for t in range(6):
                    pieces(2 * t, r, rslot)
                    if t == 5:
                        stage_block(h + 1)
                        stage_k(0, h, slot)
                    head_job(t, h, slot)
                    pieces(2 * t + 1, r, rslot)

            stage_block(0)
            pool.wait_ge(ckt_ready, 1)
            head(0, None, 0, None)
            with pool.Fori(1, RH) as h:
                head(h, h - 1, h % 2, (h - 1) % 2)
            pool.wait_ge(att_staged, RH + 1)
            pool.wait_ge(cache_in, 32)
            nc.gpsimd.tensor_copy(k_st[:, 0:P], ckt[:, :])
            nc.gpsimd.tensor_copy(v_st[:, 0, :], cva[:, :]).then_inc(cache_staged, 1)
            for place_ in range(12):
                pieces(place_, RH - 1, (RH - 1) % 2)
            pool.wait_ge(unit_done, U_MRG2)
            pool.wait_ge(x_saved, 16)
            pool.dma_start(res[:, :, :].rearrange("p k n -> p (k n)"), scratch).then_inc(x_back, 16)
            pool.wait_ge(unit_done, U_OUT)
            nc.gpsimd.memset(sqacc[:, ROWS:PADROWS], 0.0)

            def add_square(src, m, fresh):
                if fresh:
                    wait(pool, sums_done, m // KD)
                    nc.gpsimd.tensor_copy(sqacc[:, 0:ROWS], src[:, :]).then_inc(sq_added, 1)
                else:
                    pool.wait_ge(sq_added, m)
                    nc.gpsimd.tensor_tensor(sqacc[:, 0:ROWS], sqacc[:, 0:ROWS], src[:, :], ALU.add).then_inc(sq_added, 1)

            def out_square(i, n, fresh=False):
                w, a = unit(J_OUT + n, 2, i)
                pool.wait_ge(acc_free[a], w + 1)
                add_square(tb, 2 * i + n, fresh)

            out_square(0, 0, fresh=True)
            out_square(0, 1)
            with pool.Fori(1, KD // 2) as i:
                out_square(i, 0)
                out_square(i, 1)
            power(1)

            pool.wait_ge(rb_ready, 2)
            def scale_tile(k):
                ap = wide[:, span(k, 1), :].rearrange("p a n -> p (a n)")
                nc.gpsimd.tensor_tensor(ap, ap, rb[:, :], ALU.mult).then_inc(scaled, 1)

            scale_tile(0)
            scale_tile(1)
            for k in range(KD):
                pool.wait_ge(sq_ready, k + 1)
                add_square((ta, tb)[k % 2], KD + k, k == 0)
                if k + 2 < KD:
                    scale_tile(k + 2)
            power(2)
            for half, (uf, jf) in enumerate(((U_FA, J_FA), (U_FB, J_FB))):
                def silu(i):
                    m = half * FTH + i
                    pool.wait_ge(silu_sg, m + 1)
                    wait(pool, f_lo, m)
                    nc.gpsimd.tensor_tensor(ta[:, :], zt[:, jf % 2, :], tb[:, :], ALU.mult).then_inc(silu_ready, 1)

                silu(0)
                with pool.Fori(1, FTH) as i:
                    silu(i)
            pool.wait_ge(sq_ready, KD + 1)
            add_square(tb, 2 * KD, True)
            with pool.Fori(1, KD) as c:
                pool.wait_ge(sq_ready, KD + 1 + c)
                add_square(tb, 2 * KD + c, False)
            power(3)
            pool.wait_ge(rb_ready, 4)
            with pool.Fori(0, KD) as k:
                scale_tile(k)
            pool.wait_ge(out_done, 16 * 6)


INPUTS = ["x_prompt", "x_sample", "p_prompt", "p_sample", "cache_attn_k", "cache_attn_v", "state_ret",
          "g_mix_pre", "w_in", "attn_sinks", "w_branch_attn", "w_branch_ret", "w_out", "g_mix_post",
          "g_ffn_pre", "w_ffn_gate", "w_ffn_up", "w_ffn_down", "g_ffn_post", "w_ple_proj", "w_ple_gate"]
OUTPUTS = [(1, SEQ, D), (1, DEC, D), (1, 1, P, KV, HD), (1, 1, P, KV, HD), (1, 1, RH, RK, RV),
           (1, 1, P, KV, HD), (1, 1, P, KV, HD), (1, 1, RH, RK, RV)]


def kernel(**inputs):
    import concourse.bacc as bacc
    from concourse.bass_utils import run_bass_kernel_spmd

    nc = bacc.Bacc("TRN2", target_bir_lowering=False, num_devices=1)
    arrays, args = {}, []
    for name in INPUTS:
        a = np.ascontiguousarray(inputs[name])
        arrays["in_" + name] = a
        args.append(nc.dram_tensor("in_" + name, a.shape, F32, kind="ExternalInput").ap())
    arrays["in_tables"] = tables()
    args.append(nc.dram_tensor("in_tables", (P, T_ALL), F32, kind="ExternalInput").ap())
    args.append(nc.dram_tensor("x_scratch", (P, KD * ROWS), F32, kind="Internal").ap())
    for i, shape in enumerate(OUTPUTS):
        args.append(nc.dram_tensor(f"out_{i}", shape, F32, kind="ExternalOutput").ap())
    encoder_layer(nc, *args)
    r = run_bass_kernel_spmd(nc, [arrays], core_ids=[0])
    return tuple(r.results[0][f"out_{i}"] for i in range(len(OUTPUTS)))
```

```python
from contextlib import ExitStack

import numpy as np
import concourse.bass as bass
from concourse import mybir

F32 = mybir.dt.float32
F32R = mybir.dt.float32r
ALU = mybir.AluOpType
ACT = mybir.ActivationFunctionType

P = 128
D = 1024
SEQ, DEC = 512, 64
ROWS = SEQ + DEC
HALF = ROWS // 2
PADROWS = ROWS + 64
RT = PADROWS // P
KD = D // P
HEADS, KV, HD = 8, 2, 64
GROUP = HEADS // KV
KW = 2 * P
RH, RK, RV = 4, 128, 256
EV = RV // P
FFN = 2816
FT = FFN // P
FTH = FT // 2
PLE = 256
KP = PLE // P
QUARTERS = 4
EPS, GN_EPS = 1e-6, 1e-5
SCALE = float(HD) ** -0.5

C_QA = 0
C_KA = C_QA + HEADS * HD
C_VA = C_KA + KV * HD
C_QR = C_VA + KV * HD
C_KR = C_QR + RH * RK
C_VR = C_KR + RH * RK
C_GR = C_VR + RH * RV
C_GA = C_GR + RH * RV
C_GB = C_GA + D

U_KV, J_KV = 0, 0
U_Q, J_Q = 2, 2
U_HEAD, J_HEAD = 6, 6
U_GATE, J_GATE = U_HEAD + 6 * RH, J_HEAD + 6 * RH
U_MRG, J_MRG = U_GATE + 8, J_GATE + 8
U_MRG2, J_MRG2 = U_MRG + 16, J_MRG + 16
U_OUT, J_OUT = U_MRG2 + 8, J_MRG2 + 8
U_P0, J_P0 = U_OUT + KD, J_OUT + KD
U_FA, J_FA = U_P0 + 1, J_P0 + 4
U_DA, J_DA = U_FA + 2 * FTH, J_FA + 2 * FTH
U_FB, J_FB = U_DA + 2 * KD, J_DA + KD
U_DB, J_DB = U_FB + 2 * FTH, J_FB + 2 * FTH
U_P1, J_P1 = U_DB + 2 * KD, J_DB + KD
U_PG, J_PG = U_P1 + 1, J_P1 + 4
DOWN_K = (6, 5)

T_ID = 0
T_DEC = T_ID + P
T_QD = T_DEC + RH * P
T_KD = T_QD + RH * P
T_KDS = T_KD + RH
T_GL = T_KDS + RH
T_GLS = T_GL + RH
T_MASK = T_GLS + RH
T_COLS = T_MASK + 3 * KW
T_ROT = T_COLS
T_ALL = T_ROT + 2 * ROWS

ADDED_OUT = KD
ADDED_X1 = ADDED_OUT + 5
ADDED_FFN = ADDED_X1 + KD

MASKED = -1.0e30


def tables():
    t = np.zeros((P, T_ALL), np.float32)
    t[:, T_ID:T_ID + P] = np.eye(P)
    m = np.arange(P, dtype=np.float64)
    for h in range(RH):
        lg = np.log1p(-np.exp2(-5.0 - h))
        diff = m[None, :] - m[:, None]
        t[:, T_DEC + h * P:T_DEC + (h + 1) * P] = np.where(
            diff >= 0, np.exp(lg * np.maximum(diff, 0)), 0.0) * RK ** -0.5
        t[:, T_QD + h * P:T_QD + (h + 1) * P] = np.exp(lg * (m + 1))[None, :]
        t[:, T_KD + h] = np.exp(lg * (P - 1 - m)) * RK ** -0.5
        t[:, T_KDS + h] = np.where(m < DEC, np.exp(lg * np.maximum(DEC - 1 - m, 0)), 0.0) * RK ** -0.5
        t[:, T_GL + h] = np.exp(lg * P)
        t[:, T_GLS + h] = np.exp(lg * DEC)
    k = np.arange(KW)[None, :]
    late = np.arange(P)[:, None] >= 64
    own = np.where(late, k >= 64, k < 192)
    t[:, T_MASK:T_MASK + KW] = np.where(own & (k >= P), 0.0, MASKED)
    t[:, T_MASK + KW:T_MASK + 2 * KW] = np.where(own, 0.0, MASKED)
    t[:, T_MASK + 2 * KW:T_MASK + 3 * KW] = np.where(k < P + DEC, 0.0, MASKED)
    half = RK // 2
    inv = (1.0 / (np.float32(10000.0) ** np.linspace(0.0, 1.0, half, dtype=np.float32))).astype(np.float32)
    ang = (np.arange(ROWS, dtype=np.float32)[None, :] * inv[:, None]).astype(np.float32)
    cos, sin = np.cos(ang.astype(np.float64)), np.sin(ang.astype(np.float64))
    t[:, T_ROT:T_ROT + ROWS] = np.concatenate([cos, cos])
    t[:, T_ROT + ROWS:T_ALL] = np.concatenate([-sin, sin])
    return t


def unit(base, step=0, i=0):
    return base // 2 + (step // 2) * i, base % 2


def span(start, size):
    return slice(start, start + size) if isinstance(start, int) else bass.ds(start, size)


def wait(eng, sem, value):
    if not (isinstance(value, int) and value <= 0):
        eng.wait_ge(sem, value)


PLACES = [
    [("att", "A", 0), ("ret", "A", 0)],
    [("att", "N", 0)],
    [("ret", "B", 0), ("ret", "A", 1), ("ret", "N", 0)],
    [("att", "B", 0), ("ret", "C", 0)],
    [("att", "C", 0), ("ret", "B", 1), ("ret", "A", 2), ("ret", "N", 1)],
    [("ret", "C", 1), ("att", "A", 1)],
    [("ret", "B", 2), ("ret", "A", 3), ("ret", "N", 2)],
    [("ret", "C", 2), ("att", "N", 1)],
    [("att", "B", 1), ("ret", "B", 3), ("ret", "A", 4), ("ret", "N", 3)],
    [("ret", "C", 3), ("att", "C", 1)],
    [("ret", "B", 4), ("ret", "N", 4), ("v", None, 0)],
    [("ret", "C", 4), ("v", None, 1)],
]


BRANCH_TILES = (0, 5, 10, GROUP + KD)


def earlier_use(c):
    return 1 if c == 0 else 2


def block_size(b):
    if isinstance(b, int) and b == 0:
        return P, P, KW, {1: P}
    if isinstance(b, int) and b == RH:
        return DEC, 0, P + DEC, {0: P, 1: DEC}
    return P, 0, KW, {0: P, 1: P}


def encoder_layer(nc, x_p, x_s, p_p, p_s, cache_k, cache_v, state_in, g_mix_pre, w_in, sinks_in,
                  w_ba, w_br, w_out, g_mix_post, g_ffn_pre, w_fg, w_fu, w_fd, g_ffn_post, w_pp, w_pg,
                  table_in, scratch, y_p, y_s, k_p, v_p, r_p, k_s, v_s, r_s):
    with ExitStack() as ctx:
        base = (nc.sbuf_base + 63) // 64 * 64
        cursor = [base]

        def place(name, shape, dt=F32, at=None):
            size = int(np.prod(shape[1:])) * 4
            if at is None:
                at = cursor[0]
                cursor[0] += (size + 31) // 32 * 32
            assert at + size <= nc.sbuf_usable_end, (name, at + size, nc.sbuf_usable_end)
            return nc.alloc_sbuf_tensor_at(name, shape, dt, offset=at)

        def sem(name):
            return ctx.enter_context(nc.semaphore(name))

        tab = place("tab", [P, T_COLS])
        rot = place("rot", [P, 2, ROWS])
        ident = tab[:, T_ID:T_ID + P]
        gains = place("gains", [P, 4 * KD])
        ones = place("ones", [P, P])
        sinks = place("sinks", [P, HEADS])
        raw = place("raw", [P, 2, KD * P])
        whi = place("whi", [P, 2, KD * P], F32R)
        wlo = place("wlo", [P, 2, KD * P], F32R)
        rb = place("rb", [P, ROWS])
        zt = place("zt", [P, 2, ROWS])
        ta = place("ta", [P, ROWS])
        tb = place("tb", [P, ROWS])
        ph = place("ph", [P, KP, ROWS], F32R)
        pl = place("pl", [P, KP, ROWS], F32R)
        rowsum = place("rowsum", [P, 8])
        rowvar = place("rowvar", [P, 8])
        rstd = place("rstd", [P, 8])
        neg_half = place("neg_half", [P, 8])
        zeros = place("zeros", [P, 8])
        preload = place("preload", [P, 1])
        slab = KD * ROWS * 4
        a_at, b_at, c_at, d_at = (cursor[0] + n * slab for n in range(4))
        e_at = d_at + slab
        f_at = e_at + slab // 2
        xh = place("xh", [P, KD, ROWS], F32R, at=a_at)
        xl = place("xl", [P, KD, ROWS], F32R, at=b_at)
        o_ret = place("o_ret", [P, KD, ROWS], at=c_at)
        sig = place("sig", [P, 4, 2, ROWS], at=d_at)
        o_att = place("o_att", [P, GROUP, ROWS], at=e_at)
        x_t = place("x_t", [P, KD, ROWS], at=d_at)
        x_row = place("x_row", [P, RT, D], at=e_at)
        p_row = place("p_row", [P, RT, PLE], at=c_at)
        g_row = place("g_row", [4 * KD, P], at=c_at + RT * PLE * 4)
        sink_row = place("sink_row", [1, HEADS], at=c_at + RT * PLE * 4 + 4 * P)
        square = place("square", [P, D], at=c_at + RT * PLE * 4 + 4 * P + 64)
        cursor[0] = f_at
        qt = place("qt", [P, GROUP, PADROWS])
        kt = place("kt", [P, P + PADROWS])
        ckt = place("ckt", [P, P])
        va = place("va", [P, RT + 1, P])
        cva = place("cva", [P, P])
        ck_row = place("ck_row", [P, P])
        k_row = place("k_row", [P, 2, P])
        q_st = place("q_st", [P, GROUP, P])
        k_st = place("k_st", [P, KW])
        v_st = place("v_st", [P, 2, P])
        prob = place("prob", [P, GROUP, KW])
        prob_t = place("prob_t", [P, 2, GROUP * P])
        top = place("top", [P, GROUP])
        neg_top = place("neg_top", [P, GROUP])
        den = place("den", [P, GROUP])
        sink_exp = place("sink_exp", [P, GROUP])
        qr = place("qr", [P, 2, PADROWS])
        kr = place("kr", [P, 2, PADROWS])
        vr = place("vr", [P, 2, RT, RV])
        gr = place("gr", [P, 2, EV, ROWS])
        rk_st = place("rk_st", [P, 2, P])
        q_dec = place("q_dec", [P, 2, P])
        s_dec = place("s_dec", [P, 2, P])
        k_dec = place("k_dec", [P, 2, P])
        o_norm = place("o_norm", [P, 2, RV])
        state_p = place("state_p", [P, RV])
        state_s = place("state_s", [P, RV])
        stats = place("stats", [P, 8])
        moments = place("moments", [P, 2])
        grstd = place("grstd", [P, 1])
        split_at = (nc.sbuf_usable_end - 3 * slab) // 32 * 32
        assert split_at >= e_at + slab
        ah = place("ah", [P, GROUP, ROWS], F32R, at=split_at)
        al = place("al", [P, GROUP, ROWS], F32R, at=split_at + slab // 2)
        rh = place("rh", [P, KD, ROWS], F32R, at=split_at + slab)
        rl = place("rl", [P, KD, ROWS], F32R, at=split_at + 2 * slab)
        yh = place("yh", [P, KD, ROWS], F32R, at=c_at)
        ml = place("ml", [P, KD, ROWS], F32R, at=e_at)
        yl = place("yl", [P, KD, ROWS], F32R, at=d_at)
        wide = place("wide", [P, KD, ROWS], at=a_at)
        res = place("res", [P, KD, ROWS], at=b_at)
        proj = place("proj", [P, KD, ROWS], at=e_at)
        cursor[0] = e_at + slab
        fh = place("fh", [P, FTH, ROWS], F32R)
        fl = place("fl", [P, FTH, ROWS], F32R)
        sq_x1 = place("sq_x1", [P, KD, ROWS], at=e_at + slab)
        sqacc = place("sqacc", [P, PADROWS])
        cursor[0] = e_at + slab
        yt = place("yt", [P, 2, ROWS])
        y_row = place("y_row", [P, 2, RT, P])
        mb = place("mb", [P, ROWS], at=e_at + slab)
        assert e_at + slab + ROWS * 4 <= split_at
        diag = tb

        acc = ctx.enter_context(nc.psum_tensor("acc", [P, 2, 2, 512], F32))
        small = ctx.enter_context(nc.psum_tensor("small", [P, 2048], F32))
        att = small[:, 0:1024]
        ret_s, ret_kt, ret_ot = small[:, 1024:1152], small[:, 1152:1280], small[:, 1280:1536]
        ret_o, ret_dl = small[:, 1536:1792], small[:, 1792:2048]

        tables_in = sem("tables_in")
        gains_in = sem("gains_in")
        ident_in, gain_in = sem("ident_in"), sem("gain_in")
        x_in = [sem(f"x_in{q}") for q in range(QUARTERS)]
        p_in = sem("p_in")
        cache_in = sem("cache_in")
        loaded = [sem("loaded0"), sem("loaded1")]
        hi_ready, lo_ready, unit_done = sem("hi_ready"), sem("lo_ready"), sem("unit_done")
        acc_free = [sem("acc_free0"), sem("acc_free1")]
        gate_sig = [sem("gate_sig0"), sem("gate_sig1")]
        ple_done = sem("ple_done")
        init_done = sem("init_done")
        gain_t, gain_ready, sinks_ready = sem("gain_t"), sem("gain_ready"), sem("sinks_ready")
        xt_psum, xt_copied, xh_ready, xl_ready = sem("xt_psum"), sem("xt_copied"), sem("xh_ready"), sem("xl_ready")
        x_saved, x_back = sem("x_saved"), sem("x_back")
        squares_ready, var_ready, rstd_ready, diag_ready = (
            sem("squares_ready"), sem("var_ready"), sem("rstd_ready"), sem("diag_ready"))
        bcast_done, rb_ready, sums_done = sem("bcast_done"), sem("rb_ready"), sem("sums_done")
        kt_ready, va_ready, kv_t, va_rows, kv_rows, ckt_ready = (
            sem("kt_ready"), sem("va_ready"), sem("kv_t"), sem("va_rows"), sem("kv_rows"), sem("ckt_ready"))
        swap_ready, cos_ready, rotated = sem("swap_ready"), sem("cos_ready"), sem("rotated")
        v_t, v_rows = sem("v_t"), sem("v_rows")
        sg_ready, g_ready = sem("sg_ready"), sem("g_ready")
        att_staged, cache_staged, att_score, att_top, att_exp, att_den, att_prob, att_t = (
            sem("att_staged"), sem("cache_staged"), sem("att_score"), sem("att_top"), sem("att_exp"), sem("att_den"),
            sem("att_prob"), sem("att_t"))
        att_t0, att_t1, att_pv, att_out = sem("att_t0"), sem("att_t1"), sem("att_pv"), sem("att_out")
        ret_kst, ret_qd, ret_A, ret_sd, ret_kd = (
            sem("ret_kst"), sem("ret_qd"), sem("ret_A"), sem("ret_sd"), sem("ret_kd"))
        ret_B, ret_state, ret_mom, ret_grstd, ret_norm, ret_C, ret_gated = (
            sem("ret_B"), sem("ret_state"), sem("ret_mom"), sem("ret_grstd"), sem("ret_norm"),
            sem("ret_C"), sem("ret_gated"))
        state_in_s, state_p_out, state_s_out = sem("state_in_s"), sem("state_p_out"), sem("state_s_out")
        branch_hi, branch_lo = sem("branch_hi"), sem("branch_lo")
        m_ready, m_hi, m_lo = sem("m_ready"), sem("m_hi"), sem("m_lo")
        sq_ready, sq_paired, sq_added, parked_scaled = sem("sq_ready"), sem("sq_paired"), sem("sq_added"), sem("parked_scaled")
        ph_ready, pl_ready = sem("ph_ready"), sem("pl_ready")
        first_scaled, scaled, res_ready, y_hi, y_lo = sem("first_scaled"), sem("scaled"), sem("res_ready"), sem("y_hi"), sem("y_lo")
        silu_sg, silu_ready, f_ready, f_hi, f_lo = (
            sem("silu_sg"), sem("silu_ready"), sem("f_ready"), sem("f_hi"), sem("f_lo"))
        y_ready, y_t, y_rows = sem("y_ready"), sem("y_t"), sem("y_rows")
        y_out = [sem("y_out0"), sem("y_out1")]
        out_done = sem("out_done")
        dve_top, dve_rot, dve_ret, dve_y = sem("dve_top"), sem("dve_rot"), sem("dve_ret"), sem("dve_y")

        act_passed, dve_passed, pool_passed = sem("act_passed"), sem("dve_passed"), sem("pool_passed")

        CREDIT = 1
        Y_CREDIT = 2

        wi = w_in[0].rearrange("(k p) n -> p k n", p=P)
        wba_v = [w_ba[0][n * 256:(n + 1) * 256, :].rearrange("(j p) n -> p j n", p=HD) for n in range(2)]
        wbr_v = w_br[0].rearrange("(k p) n -> p k n", p=P)
        wo_v = w_out[0].rearrange("(k p) n -> p k n", p=P)
        wfg_v = w_fg[0].rearrange("(k p) n -> p k n", p=P)
        wfu_v = w_fu[0].rearrange("(k p) n -> p k n", p=P)
        wfd_v = w_fd[0].rearrange("(k p) n -> p k n", p=P)
        wpp_v = w_pp[0].rearrange("(k p) n -> p k n", p=P)
        wpg_v = w_pg[0].rearrange("(k p) n -> p k n", p=P)

        def acc_of(a):
            return acc[:, a, :, 0:HALF]

        def halves(ap):
            return ap.rearrange("p (h n) -> p h n", h=2)

        block = ctx.enter_context(nc.Block())

        @block.sync
        def _(sp):
            def load(vs, parts):
                v, s = vs
                wait(sp, lo_ready, 2 * v + s - 1)
                assert len(parts) == 2
                for dst, src in parts:
                    sp.dma_start(dst, src).then_inc(loaded[s], 16)

            def columns(vs, view, col, k0=0, ks=KD):
                first = (ks + 1) // 2
                s = vs[1]
                slot = raw[:, s, :].rearrange("p (k n) -> p k n", n=P)
                load(vs, [(slot[:, 0:first, :], view[:, k0:k0 + first, span(col, P)]),
                          (slot[:, first:ks, :], view[:, k0 + first:k0 + ks, span(col, P)])])

            def q_columns(vs, j):
                slot = raw[:, vs[1], :].rearrange("p (k n) -> p k n", n=P)
                load(vs, [(slot[:, :, 0:HD], wi[:, :, span(C_QA + HD * j, HD)]),
                          (slot[:, :, HD:P], wi[:, :, span(C_QA + HD * (j + GROUP), HD)])])

            def att_columns(vs, col):
                slot = raw[:, vs[1], 0:GROUP * P].rearrange("p (k n) -> p k n", n=P)
                load(vs, [(slot[64 * n:64 * n + 64], wba_v[n][:, :, span(col, P)]) for n in range(2)])

            def ple_columns(vs, n):
                slot = raw[:, vs[1], :].rearrange("p (k n) -> p k n", n=4 * P)
                load(vs, [(slot[:, k, :], wpp_v[:, k, n * 4 * P:(n + 1) * 4 * P]) for k in range(KP)])

            def x_quarter(q):
                cols = slice(q * D // QUARTERS, (q + 1) * D // QUARTERS)
                sp.dma_start(x_row[:, 0:RT - 1, cols], x_p[0].rearrange("(r p) n -> p r n", p=P)[:, :, cols]
                             ).then_inc(x_in[q], 16)
                sp.dma_start(x_row[0:DEC, RT - 1, cols], x_s[0][:, cols]).then_inc(x_in[q], 16)

            x_quarter(0)
            x_quarter(1)
            columns(unit(U_KV), wi, C_KA)
            x_quarter(2)
            columns(unit(U_KV + 1), wi, C_VA)
            x_quarter(3)
            with sp.Fori(0, GROUP // 2) as i:
                for n in range(2):
                    q_columns(unit(U_Q + n, 2, i), 2 * i + n)
            with sp.Fori(0, RH) as h:
                for n, col in enumerate((C_QR + RK * h, C_GR + RV * h, C_KR + RK * h,
                                         C_VR + RV * h, C_VR + RV * h + P, C_GR + RV * h + P)):
                    columns(unit(U_HEAD + n, 6, h), wi, col)
            with sp.Fori(0, 4) as c:
                columns(unit(U_GATE, 2, c), wi, C_GA + P * c)
                columns(unit(U_GATE + 1, 2, c), wi, C_GB + P * c)
            with sp.Fori(0, 4) as c:
                att_columns(unit(U_MRG, 4, c), P * c)
                columns(unit(U_MRG + 1, 4, c), wbr_v, P * c)
                columns(unit(U_MRG + 2, 4, c), wi, C_GA + 4 * P + P * c)
                columns(unit(U_MRG + 3, 4, c), wi, C_GB + 4 * P + P * c)
            with sp.Fori(0, 4) as c:
                att_columns(unit(U_MRG2, 2, c), 4 * P + P * c)
                columns(unit(U_MRG2 + 1, 2, c), wbr_v, 4 * P + P * c)
            with sp.Fori(0, KD // 2) as i:
                for n in range(2):
                    columns(unit(U_OUT + n, 2, i), wo_v, 2 * P * i + n * P)
            ple_columns(unit(U_P0), 0)
            for half, (uf, ud) in enumerate(((U_FA, U_DA), (U_FB, U_DB))):
                with sp.Fori(0, FTH) as i:
                    columns(unit(uf, 2, i), wfg_v, half * FTH * P + P * i)
                    columns(unit(uf + 1, 2, i), wfu_v, half * FTH * P + P * i)
                with sp.Fori(0, KD) as c:
                    columns(unit(ud, 2, c), wfd_v, P * c, k0=half * FTH, ks=DOWN_K[0])
                    columns(unit(ud + 1, 2, c), wfd_v, P * c, k0=half * FTH + DOWN_K[0], ks=DOWN_K[1])
            ple_columns(unit(U_P1), 1)
            with sp.Fori(0, KD // 2) as i:
                for n in range(2):
                    columns(unit(U_PG + n, 2, i), wpg_v, 2 * P * i + n * P)
            for c in range(KD):
                sp.wait_ge(y_rows, c + 1 + Y_CREDIT)
                sp.dma_start(y_p[0].rearrange("(r p) n -> p r n", p=P)[:, :, c * P:(c + 1) * P],
                             y_row[:, c % 2, 0:RT - 1, :]).then_inc(y_out[c % 2], 16)
                sp.dma_start(y_s[0][:, c * P:(c + 1) * P], y_row[0:DEC, c % 2, RT - 1, :]).then_inc(y_out[c % 2], 16)
            for n in range(2):
                sp.wait_ge(y_out[n], 32 * KD // 2)

        @block.tensor
        def _(pe):
            def products(s, a, ks, rhs_h, rhs_l, first, last, tile_at):
                ins = None
                for n, k in enumerate(ks):
                    at = tile_at(k)
                    for m, (w, x) in enumerate(((whi, rhs_h), (whi, rhs_l), (wlo, rhs_h))):
                        for hf in range(2):
                            ins = nc.tensor.matmul(
                                acc[:, a, hf, 0:HALF], w[:, s, at:at + P], x(k)[:, hf * HALF:(hf + 1) * HALF],
                                start=first and n == 0 and m == 0, stop=last and n == len(ks) - 1 and m == 2)
                return ins

            def run_unit(vs, wa, rhs, ks=KD, k0=0, first=True, last=True, ready=None,
                         between=None):
                (v, s), (w, a) = vs, wa
                if first:
                    wait(pe, acc_free[a], w)
                pe.wait_ge(lo_ready, 2 * v + s + 1)
                rh_, rl_ = rhs
                if between is not None:
                    for part in (range(ks // 2), range(ks // 2, ks)):
                        ins = products(s, a, part, lambda k: rh_[:, k, :], lambda k: rl_[:, k, :],
                                       part[0] == 0, part[-1] == ks - 1, lambda k: k * P)
                        if part[0] == 0:
                            between()
                elif ready is None:
                    ins = products(s, a, range(ks), lambda k: rh_[:, k0 + k, :], lambda k: rl_[:, k0 + k, :],
                                   first, last, lambda k: k * P)
                else:
                    for k in range(ks):
                        ready(k0 + k)
                        ins = products(s, a, [k], lambda k: rh_[:, k0 + k, :], lambda k: rl_[:, k0 + k, :],
                                       first and k == 0, last and k == ks - 1, lambda k: k * P)
                ins.then_inc(unit_done, 1)

            def run_pair(units, jobs, rhs, ready, lag, before=None, tail=None):
                for step in range(KD + lag):
                    for n, k in ((0, step), (1, step - lag)):
                        if not 0 <= k < KD:
                            continue
                        (v, s), (w, a) = units[n], jobs[n]
                        if n == 0:
                            if before is not None:
                                before(k)
                            ready(k)
                        if k == 0:
                            wait(pe, acc_free[a], w)
                            pe.wait_ge(lo_ready, 2 * v + s + 1)
                        ins = products(s, a, [k], lambda k: rhs[0][:, k, :], lambda k: rhs[1][:, k, :],
                                       k == 0, k == KD - 1, lambda k: k * P)
                        if k == KD - 1:
                            ins.then_inc(unit_done, 1)
                            if n == 0 and tail is not None:
                                tail()

            def run_ple(u, j, n, behind):
                v, s = unit(u)
                pe.wait_ge(lo_ready, 2 * v + s + 1)
                pe.wait_ge(pl_ready, KP)
                for c in range(4):
                    w, a = unit(j + c)
                    wait(pe, acc_free[a], w)
                    ins = products(s, a, range(KP), lambda k: ph[:, k, :], lambda k: pl[:, k, :],
                                   True, True, lambda k: k * 4 * P + c * P)
                    ins.then_inc(unit_done if c == 3 else ple_done, 1)
                    if c in behind:
                        behind[c]()

            def row_factor(n):
                for r in range(RT):
                    size = P if r < RT - 1 else DEC
                    pe.wait_ge(diag_ready, RT * n + r + 1)
                    ins = nc.tensor.matmul(small[:, r * P:r * P + size], ones[0:size, :],
                                           diag[0:size, P * r:P * r + size], start=True, stop=True)
                    ins.then_inc(bcast_done, 1)

            def row_sums(added):
                pe.wait_ge(sq_added, added)
                for r in range(RT):
                    ins = nc.tensor.matmul(ret_s[:, r:r + 1], sqacc[:, r * P:(r + 1) * P], ones[:, 0:1],
                                           start=True, stop=True)
                ins.then_inc(sums_done, 1)

            pe.wait_ge(ident_in, 16)
            pe.wait_ge(gain_in, 16)
            pe.wait_ge(init_done, 1)
            nc.tensor.transpose(small[:, 1536:1536 + KD], g_row[0:KD, :], ident[0:KD, 0:KD]).then_inc(gain_t, 1)
            pe.wait_ge(gain_ready, 1)

            def x_transposes(k):
                if k < KD:
                    pe.wait_ge(x_in[k * QUARTERS // KD], 32)
                else:
                    pe.wait_ge(p_in, 32)
                wait(pe, xt_copied, k - 1)
                at = 1024 * (k % 2)
                src, col = (x_row, k * P) if k < KD else (p_row, (k - KD) * P)
                for r in range(RT):
                    size = P if r < RT - 1 else DEC
                    ins = nc.tensor.transpose(small[:, at + r * P:at + r * P + size],
                                              src[0:size, r, col:col + P], ident[0:size, 0:size])
                ins.then_inc(xt_psum, 1)

            def first_factor():
                pe.wait_ge(xt_copied, KD)
                row_factor(0)

            for k in range(4):
                x_transposes(k)
            run_pair((unit(U_KV), unit(U_KV + 1)), (unit(J_KV), unit(J_KV + 1)), (xh, xl),
                     ready=lambda k: pe.wait_ge(xl_ready, k + 1), lag=3,
                     before=lambda k: x_transposes(k + 3) if 0 < k < KD - 3 else None, tail=first_factor)
            pe.wait_ge(rb_ready, 1)
            x_transposes(KD)
            x_transposes(KD + 1)
            for n in range(2):
                run_unit(unit(U_Q + n), unit(J_Q + n), (xh, xl))
            pe.wait_ge(va_ready, 1)
            pe.wait_ge(kt_ready, 1)
            pe.wait_ge(cache_in, 32)
            pe.wait_ge(gains_in, 16 * 4)
            pe.wait_ge(xt_copied, KD + KP)
            vt_tmp = prob[:, 0:3, :].rearrange("p j n -> p (j n)")
            for r in range(RT):
                size = P if r < RT - 1 else DEC
                nc.tensor.transpose(att[0:size, r * P:(r + 1) * P], vt_tmp[:, r * P:r * P + size], ident)
            nc.tensor.transpose(small[:, 1024:1152], kt[:, P + SEQ - P:P + SEQ], ident)
            nc.tensor.transpose(small[0:DEC, 1152:1280], kt[:, P + SEQ:P + ROWS], ident)
            nc.tensor.transpose(small[:, 1664:1664 + 4 * KD], g_row[:, :], ident[0:4 * KD, 0:4 * KD])
            nc.tensor.matmul(small[:, 1728:1728 + HEADS], ones[0:1, :], sink_row[0:1, :], start=True, stop=True)
            nc.tensor.transpose(small[:, 1536:1664], ck_row[:, :], ident).then_inc(kv_t, 1)
            for n in (2, 3):
                run_unit(unit(U_Q + n), unit(J_Q + n), (xh, xl))

            def att_piece(piece, g, b):
                n = 2 * b + g
                nq, k0, k1, tiles = block_size(b)
                if piece == "A":
                    if isinstance(b, int) and b == 0 and g == 0:
                        pe.wait_ge(va_rows, 2)
                    pe.wait_ge(att_staged, b + 1)
                    if isinstance(b, int) and b == RH:
                        pe.wait_ge(cache_staged, 1)
                    wait(pe, att_out, n)
                    wait(pe, v_rows, 2 * b)
                    for j in range(GROUP):
                        ins = nc.tensor.matmul(att[0:nq, j * KW + k0:j * KW + k1], q_st[64 * g:64 * g + 64, j, 0:nq],
                                               k_st[64 * g:64 * g + 64, k0:k1], start=True, stop=True)
                    ins.then_inc(att_score, 1)
                elif piece == "B":
                    pe.wait_ge(att_prob, n + 1)
                    pe.wait_ge(att_top, n + 1)
                    for t, nk in tiles.items():
                        for j in range(GROUP):
                            ins = nc.tensor.transpose(att[0:nk, t * 512 + j * nq:t * 512 + (j + 1) * nq],
                                                      prob[0:nq, j, t * P:t * P + nk], ident[0:nq, 0:nq])
                    ins.then_inc(att_t, 1)
                elif piece == "C":
                    pe.wait_ge(att_t0, n + 1)
                    pe.wait_ge(att_t1, n + 1)
                    for t, nk in tiles.items():
                        ins = nc.tensor.matmul(att[64 * g:64 * g + 64, 0:GROUP * nq], v_st[0:nk, t, 64 * g:64 * g + 64],
                                               prob_t[0:nk, t, 0:GROUP * nq], start=t == min(tiles), stop=t == 1)
                    ins.then_inc(att_pv, 1)

            def ret_piece(piece, c, r, slot):
                n = 5 * r + c
                if piece == "A":
                    pe.wait_ge(ret_sd, n + CREDIT)
                    pe.wait_ge(ret_kd, n + CREDIT)
                    pe.wait_ge(ret_gated, 5 * r + max(0, c - 1) + CREDIT)
                    pe.wait_ge(rotated, 2 * r + 2)
                    pe.wait_ge(ret_kst, n + 1 + CREDIT)
                    nc.tensor.matmul(ret_s, rk_st[:, c % 2, :], qr[:, slot, c * P:(c + 1) * P] if isinstance(slot, int)
                                     else qr[:, bass.ds(slot, 1), c * P:(c + 1) * P].rearrange("p a n -> p (a n)"),
                                     start=True, stop=True)
                    nc.tensor.transpose(ret_kt, rk_st[:, c % 2, :], ident).then_inc(ret_A, 1)
                elif piece == "B":
                    pe.wait_ge(ret_sd, n + 1 + CREDIT)
                    pe.wait_ge(ret_kd, n + 1 + CREDIT)
                    pe.wait_ge(ret_qd, n + 1 + CREDIT)
                    pe.wait_ge(ret_state, n + CREDIT)
                    pe.wait_ge(ret_norm, n + CREDIT)
                    pe.wait_ge(v_rows, 2 * r + 2)
                    v = vr[:, slot, c, :] if isinstance(slot, int) else \
                        vr[:, bass.ds(slot, 1), c, :].rearrange("p a n -> p (a n)")
                    if c == RT - 1:
                        pe.wait_ge(state_in_s, 16 * (r + 1))
                    nc.tensor.matmul(ret_o, s_dec[:, c % 2, :], v, start=True, stop=c == 0)
                    if c > 0:
                        nc.tensor.matmul(ret_o, q_dec[:, c % 2, :], (state_s if c == RT - 1 else state_p)[:, :],
                                         start=False, stop=True)
                    nc.tensor.matmul(ret_dl, k_dec[:, c % 2, :], v, start=True, stop=True).then_inc(ret_B, 1)
                elif piece == "C":
                    pe.wait_ge(ret_norm, n + 1 + CREDIT)
                    pe.wait_ge(ret_gated, n + CREDIT)
                    pe.wait_ge(ret_sd, 5 * r + min(c + 2, RT) + CREDIT)
                    pe.wait_ge(ret_kd, 5 * r + min(c + 2, RT) + CREDIT)
                    for e in range(EV):
                        ins = nc.tensor.transpose(ret_ot[:, e * P:(e + 1) * P], o_norm[:, c % 2, e * P:(e + 1) * P], ident)
                    ins.then_inc(ret_C, 1)

            def v_transposes(e, h):
                w, a = unit(J_HEAD + (3, 4)[e], 6, h)
                pe.wait_ge(acc_free[a], w + 1)
                wait(pe, v_rows, 2 * h + e)
                pe.wait_ge(att_t1, 2 * h + 2)
                pe.wait_ge(att_out, 2 * h + 2)
                for r in range(RT - 1):
                    nc.tensor.transpose(att[:, r * P:(r + 1) * P], zt[:, a, r * P:(r + 1) * P], ident)
                nc.tensor.transpose(att[0:DEC, SEQ:SEQ + P], zt[:, a, SEQ:ROWS], ident).then_inc(v_t, 1)

            def pieces(place, h, b, r, slot):
                for kind, piece, c in PLACES[place]:
                    if kind == "att":
                        att_piece(piece, c, b)
                    elif kind == "ret" and r is not None:
                        ret_piece(piece, c, r, slot)
                    elif kind == "v" and h is not None:
                        v_transposes(c, h)

            def six_jobs(u, j, per, i, h, b, r, slot):
                for t in range(6):
                    run_unit(unit(u + t, per, i), unit(j + t, per, i), (xh, xl),
                             between=lambda: pieces(2 * t, h, b, r, slot))
                    pieces(2 * t + 1, h, b, r, slot)

            pe.wait_ge(ckt_ready, 1)
            pe.wait_ge(kv_rows, 1)
            six_jobs(U_HEAD, J_HEAD, 6, 0, 0, 0, None, None)
            with pe.Fori(1, RH) as h:
                six_jobs(U_HEAD, J_HEAD, 6, h, h, h, h - 1, (h - 1) % 2)
            six_jobs(U_GATE, J_GATE, 6, 0, None, RH, RH - 1, (RH - 1) % 2)
            for n in (6, 7):
                run_unit(unit(U_GATE + n), unit(J_GATE + n), (xh, xl))

            def merge(u, j, per, c, ready=None):
                run_unit(unit(u, per, c), unit(j, per, c), (ah, al), ks=GROUP, ready=ready and ready[0])
                run_unit(unit(u + 1, per, c), unit(j + 1, per, c), (rh, rl), ready=ready and ready[1])

            merge(U_MRG, J_MRG, 4, 0, ready=(lambda k: pe.wait_ge(branch_lo, k + 1),
                                             lambda k: pe.wait_ge(branch_lo, GROUP + k + 1)))
            for n in (2, 3):
                run_unit(unit(U_MRG + n), unit(J_MRG + n), (xh, xl))
            with pe.Fori(1, 4) as c:
                merge(U_MRG, J_MRG, 4, c)
                for n in (2, 3):
                    run_unit(unit(U_MRG + n, 4, c), unit(J_MRG + n, 4, c), (xh, xl))
            with pe.Fori(0, 4) as c:
                merge(U_MRG2, J_MRG2, 2, c)
            run_unit(unit(U_OUT), unit(J_OUT), (yh, ml), ready=lambda k: pe.wait_ge(m_lo, k + 1))
            run_unit(unit(U_OUT + 1), unit(J_OUT + 1), (yh, ml))
            with pe.Fori(1, KD // 2) as i:
                for n in range(2):
                    run_unit(unit(U_OUT + n, 2, i), unit(J_OUT + n, 2, i), (yh, ml))
            run_ple(U_P0, J_P0, 0, behind={1: lambda: row_sums(ADDED_OUT), 2: lambda: row_factor(1)})
            for half, (uf, jf, ud, jd) in enumerate(((U_FA, J_FA, U_DA, J_DA), (U_FB, J_FB, U_DB, J_DB))):
                if half == 0:
                    run_pair((unit(uf), unit(uf + 1)), (unit(jf), unit(jf + 1)), (yh, yl),
                             ready=lambda k: pe.wait_ge(y_lo, k + 1), lag=3)
                    run_unit(unit(uf + 2), unit(jf + 2), (yh, yl), between=lambda: row_sums(ADDED_X1))
                    row_factor(2)
                    run_unit(unit(uf + 3), unit(jf + 3), (yh, yl))
                else:
                    run_unit(unit(uf), unit(jf), (yh, yl))
                    run_unit(unit(uf + 1), unit(jf + 1), (yh, yl))
                with pe.Fori(2 - half, FTH) as i:
                    run_unit(unit(uf, 2, i), unit(jf, 2, i), (yh, yl))
                    run_unit(unit(uf + 1, 2, i), unit(jf + 1, 2, i), (yh, yl))

                def down(c0, i, n, ready=None):
                    ja = unit(jd + n, 2, i)
                    run_unit(unit(ud + 2 * n, 4, i), ja, (fh, fl), ks=DOWN_K[0], last=False, ready=ready)
                    run_unit(unit(ud + 2 * n + 1, 4, i), ja, (fh, fl), ks=DOWN_K[1], k0=DOWN_K[0], first=False,
                             ready=ready)

                down(0, 0, 0, ready=lambda k: pe.wait_ge(f_lo, half * FTH + k + 1))
                down(0, 0, 1)
                with pe.Fori(1, KD // 2) as i:
                    down(0, i, 0)
                    down(0, i, 1)
            run_ple(U_P1, J_P1, 1, behind={1: lambda: row_sums(ADDED_FFN), 2: lambda: row_factor(3)})

            def y_transposes(c, n):
                pe.wait_ge(y_ready, c + 1)
                pe.wait_ge(y_rows, c - 1 + Y_CREDIT)
                at = 1024 * n
                for r in range(RT):
                    size = P if r < RT - 1 else DEC
                    ins = nc.tensor.transpose(small[0:size, at + r * P:at + (r + 1) * P],
                                              yt[:, n, r * P:r * P + size], ident)
                ins.then_inc(y_t, 1)

            run_pair((unit(U_PG), unit(U_PG + 1)), (unit(J_PG), unit(J_PG + 1)), (yh, yl),
                     ready=lambda k: pe.wait_ge(y_lo, KD + k + 1), lag=3)
            with pe.Fori(1, KD // 2) as i:
                run_unit(unit(U_PG, 2, i), unit(J_PG, 2, i), (yh, yl))
                y_transposes(2 * i - 2, 0)
                run_unit(unit(U_PG + 1, 2, i), unit(J_PG + 1, 2, i), (yh, yl))
                y_transposes(2 * i - 1, 1)
            y_transposes(KD - 2, 0)
            y_transposes(KD - 1, 1)

        @block.scalar
        def _(act):
            def split_hi(vs, n=KD * P):
                v, s = vs
                act.wait_ge(loaded[s], 32 * (v + 1))
                wait(act, unit_done, 2 * v + s - 1)
                nc.scalar.activation(whi[:, s, 0:n], raw[:, s, 0:n], ACT.Copy).then_inc(hi_ready, 1)

            def settled():
                act.sem_inc(act_passed, 1)

            act.dma_start(ident, table_in[:, T_ID:T_ID + P]).then_inc(ident_in, 16)
            act.dma_start(g_row[0:KD, :], g_mix_pre[0].rearrange("(k p) -> k p", p=P)).then_inc(gain_in, 16)
            for s_ in (state_p_out, state_s_out):
                act.sem_inc(s_, 16 * CREDIT)

            def row_squares(r):
                size = P if r < RT - 1 else DEC
                for q in range(QUARTERS):
                    act.wait_ge(x_in[q], 32)
                wait(act, squares_ready, r)
                nc.scalar.activation(square[0:size, :], x_row[0:size, r, :], ACT.Square,
                                     accum_out=rowsum[0:size, r:r + 1]).then_inc(squares_ready, 1)

            act.wait_ge(init_done, 1)
            nc.scalar.activation(preload[:, :], zeros[:, 0:1], ACT.Copy)
            act.wait_ge(gain_ready, 1)
            for k in range(KD):
                act.wait_ge(xt_copied, k + 1)
                nc.scalar.activation(xh[:, k, :], x_t[:, k, :], ACT.Copy,
                                     scale=gains[:, k:k + 1]).then_inc(xh_ready, 1)
                if k in (1, 4):
                    split_hi(unit(k // 4))
                if k >= KD // 2:
                    row_squares(k - KD // 2)
            row_squares(RT - 1)

            def row_factor(n):
                act.wait_ge(bcast_done, RT * (n + 1))
                nc.scalar.activation(rb[:, :], small[:, 0:ROWS], ACT.Copy).then_inc(rb_ready, 1)

            split_hi(unit(U_Q))
            row_factor(0)
            split_hi(unit(U_Q + 1))
            for k in range(KP):
                act.wait_ge(xt_copied, KD + k + 1)
                nc.scalar.activation(ph[:, k, :], (ta, tb)[k][:, :], ACT.Copy).then_inc(ph_ready, 1)
            split_hi(unit(U_Q + 2))
            split_hi(unit(U_Q + 3))
            act.wait_ge(kv_t, 1)
            nc.scalar.activation(va[0:DEC, RT, :], att[0:DEC, SEQ:SEQ + P], ACT.Copy).then_inc(va_rows, 1)
            nc.scalar.activation(k_row[:, 0, :], small[:, 1024:1152], ACT.Copy)
            nc.scalar.activation(k_row[0:DEC, 1, :], small[0:DEC, 1152:1280], ACT.Copy).then_inc(kv_rows, 1)
            split_hi(unit(U_HEAD))
            split_hi(unit(U_HEAD + 1))

            def att_piece(piece, g, b):
                n = 2 * b + g
                nq, k0, k1, tiles = block_size(b)
                if piece == "A":
                    act.wait_ge(att_top, n + 1)
                    for j in range(GROUP):
                        nc.scalar.activation(prob[0:nq, j, k0:k1], prob[0:nq, j, k0:k1], ACT.Exp,
                                             bias=neg_top[0:nq, j:j + 1], accum_out=den[0:nq, j:j + 1])
                    nc.scalar.activation(sink_exp[0:nq, :], top[0:nq, :], ACT.Exp).then_inc(att_exp, 1)
                elif piece == "B":
                    if 0 in tiles:
                        act.wait_ge(att_t, n + 1)
                        nc.scalar.activation(prob_t[:, 0, 0:GROUP * nq], att[:, 0:GROUP * nq], ACT.Copy).then_inc(att_t0, 1)
                    else:
                        act.sem_inc(att_t0, 1)
                elif piece == "C":
                    act.wait_ge(att_pv, n + 1)
                    src = att[64 * g:64 * g + 64, 0:GROUP * nq].rearrange("p (j n) -> p j n", j=GROUP)
                    settled()
                    nc.scalar.activation(o_att[64 * g:64 * g + 64, :, span(P * b, nq)], src, ACT.Copy).then_inc(att_out, 1)

            def head_job(t, h):
                w, a = unit(J_HEAD + t, 6, h)
                if t in (0, 2):
                    act.wait_ge(acc_free[a], w + 1)
                    m = 2 * h + t // 2
                    wait(act, rotated, m)
                    wait(act, g_ready, m)
                    nc.scalar.activation(tb[0:64, :], zt[64:128, a, :], ACT.Copy)
                    nc.scalar.activation(tb[64:128, :], zt[0:64, a, :], ACT.Copy).then_inc(swap_ready, 1)
                elif t in (1, 5):
                    act.wait_ge(acc_free[a], w + 1)
                    m = 2 * h + t // 5
                    wait(act, g_ready, m)
                    act.wait_ge(rotated, m + 1)
                    nc.scalar.activation(tb[:, :], zt[:, a, :], ACT.Sigmoid).then_inc(sg_ready, 1)

            def state_piece(piece, c, r):
                if piece == "A" and c == 1:
                    act.wait_ge(state_s_out, 16 * (r + CREDIT))
                    settled()
                    act.dma_start(state_s[:, :], state_in[0, 0, span(r, 1)].rearrange("a d e -> d (a e)")
                                  ).then_inc(state_in_s, 16)
                elif piece == "B" and c >= RT - 2:
                    out, st, done = ((r_p, state_p, state_p_out), (r_s, state_s, state_s_out))[c - (RT - 2)]
                    act.wait_ge(ret_state, 5 * r + c + 1 + CREDIT)
                    settled()
                    act.dma_start(out[0, 0, span(r, 1)].rearrange("a d e -> d (a e)"), st[:, :]).then_inc(done, 16)

            def pieces(place, b, r):
                for kind, piece, c in PLACES[place]:
                    if kind == "att":
                        att_piece(piece, c, b)
                    elif kind == "ret" and r is not None:
                        state_piece(piece, c, r)

            def head(h, b, r):
                for t in range(6):
                    pieces(2 * t, b, r)
                    split_hi(unit(U_HEAD + t + 2, 6, h))
                    head_job(t, h)
                    pieces(2 * t + 1, b, r)

            head(0, 0, None)
            with act.Fori(1, RH) as h:
                head(h, h, h - 1)

            def gate(w, a, dst):
                act.wait_ge(acc_free[a], w + 1)
                settled()
                nc.scalar.activation(dst, zt[:, a, :], ACT.Sigmoid).then_inc(gate_sig[a], 1)

            act.wait_ge(att_staged, RH + 1)
            act.wait_ge(ckt_ready, 1)
            act.wait_ge(cache_in, 32)
            nc.scalar.activation(k_st[:, 0:P], ckt[:, :], ACT.Copy)
            nc.scalar.activation(v_st[:, 0, :], cva[:, :], ACT.Copy).then_inc(cache_staged, 1)

            def branch_parts(tiles):
                for k in tiles:
                    dst, src = (ah[:, k, :], o_att[:, k, :]) if k < GROUP else \
                        (rh[:, k - GROUP, :], o_ret[:, k - GROUP, :])
                    nc.scalar.activation(dst, src, ACT.Copy).then_inc(branch_hi, 1)

            for t in range(8):
                if t < 6:
                    pieces(2 * t, RH, RH - 1)
                    split_hi(unit(U_GATE + t + 2))
                else:
                    split_hi(unit(U_MRG + t - 6), n=(GROUP if t == 6 else KD) * P)
                w, a = unit(J_GATE + t)
                if t == 0:
                    act.wait_ge(x_saved, 16)
                gate(w, a, sig[:, t // 2, t % 2, :])
                if t < 6:
                    pieces(2 * t + 1, RH, RH - 1)
                if t == 5:
                    act.wait_ge(att_pv, 2 * (RH + 1))
                    act.wait_ge(att_out, 2 * (RH + 1))
                    act.wait_ge(ret_C, 5 * RH + CREDIT)
                    act.wait_ge(ret_gated, 5 * RH + CREDIT)
                    act.wait_ge(state_p_out, 16 * (RH + CREDIT))
                    act.wait_ge(state_s_out, 16 * (RH + CREDIT))
                    act.wait_ge(out_done, 16 * 6)
                if t >= 5:
                    branch_parts(range(BRANCH_TILES[t - 5], BRANCH_TILES[t - 4]))

            def merged(c):
                act.wait_ge(m_ready, c + 1)
                settled()
                nc.scalar.activation(yh[:, span(c, 1), :].rearrange("p a n -> p (a n)"), ta[:, :], ACT.Copy).then_inc(m_hi, 1)

            with act.Fori(0, 4) as c:
                for n in range(4):
                    nxt = (2, 3, 4, 5)[n]
                    split_hi(unit(U_MRG + nxt, 4, c), n=(GROUP if n == 2 else KD) * P)
                    if n == 1:
                        merged(c)
                    if n >= 2:
                        w, a = unit(J_MRG + n, 4, c)
                        act.wait_ge(m_ready, c + 1)
                        gate(w, a, sig[:, span(c, 1), n - 2, :].rearrange("p a n -> p (a n)"))
            with act.Fori(0, 3) as c:
                split_hi(unit(U_MRG2 + 2, 2, c), n=GROUP * P)
                split_hi(unit(U_MRG2 + 3, 2, c))
                merged(c + 4)
            split_hi(unit(U_OUT))
            split_hi(unit(U_OUT + 1))
            merged(7)

            def store_square(i, n):
                w, a = unit(J_OUT + n, 2, i)
                act.wait_ge(unit_done, U_OUT + n + 1 + 2 * i)
                settled()
                nc.scalar.activation(halves(wide[:, span(2 * i + n, 1), :].rearrange("p a n -> p (a n)")), acc_of(a),
                                     ACT.Copy)
                wait(act, sq_added, 2 * i + n)
                nc.scalar.activation(halves(tb[:, :]), acc_of(a), ACT.Square).then_inc(acc_free[a], 1)
                split_hi(unit(U_OUT + 2 + n, 2, i))

            store_square(0, 0)
            store_square(0, 1)
            with act.Fori(1, KD // 2) as i:
                store_square(i, 0)
                store_square(i, 1)

            def split_res(m, gain):
                def two(i):
                    for n in range(2):
                        k = 2 * i + n
                        act.wait_ge(res_ready, KD * m + k + 1)
                        settled()
                        dst = yh[:, span(k, 1), :].rearrange("p a n -> p (a n)")
                        src = res[:, span(k, 1), :].rearrange("p a n -> p (a n)")
                        if gain is None:
                            nc.scalar.activation(dst, src, ACT.Copy).then_inc(y_hi, 1)
                        else:
                            nc.scalar.activation(dst, src, ACT.Copy, scale=gains[:, span(gain + k, 1)]).then_inc(y_hi, 1)
                            sq = sq_x1[:, span(k, 1), :].rearrange("p a n -> p (a n)")
                            nc.scalar.activation(sq, src, ACT.Square).then_inc(sq_ready, 1)

                with act.Fori(0, KD // 2) as i:
                    two(i)

            row_factor(1)
            split_hi(unit(U_FA + 1))
            split_res(0, 2 * KD)
            for n in (2, 3, 4):
                split_hi(unit(U_FA + n))
            row_factor(2)
            for half, (uf, jf, ud, jd) in enumerate(((U_FA, J_FA, U_DA, J_DA), (U_FB, J_FB, U_DB, J_DB))):
                def ffn(i, ahead):
                    if ahead[0] is not None:
                        split_hi(*ahead[0])
                    if half == 0 and isinstance(i, int) and i == 0:
                        act.wait_ge(parked_scaled, 1)
                    else:
                        act.wait_ge(acc_free[jf % 2], unit(jf, 2, i)[0] + 1)
                    nc.scalar.activation(tb[:, :], zt[:, jf % 2, :], ACT.Sigmoid).then_inc(silu_sg, 1)
                    if ahead[1] is not None:
                        split_hi(*ahead[1])
                    act.wait_ge(f_ready, half * FTH + i + 1)
                    settled()
                    nc.scalar.activation(fh[:, span(i, 1), :].rearrange("p a n -> p (a n)"), ta[:, :], ACT.Copy).then_inc(f_hi, 1)

                if half == 0:
                    ffn(0, (None, None))
                    ffn(1, (None, (unit(uf + 5),)))
                with act.Fori(2 * (1 - half), FTH - 1) as i:
                    ffn(i, ((unit(uf + 2, 2, i),), (unit(uf + 3, 2, i),)))
                ffn(FTH - 1, ((unit(ud), DOWN_K[0] * P), (unit(ud + 1), DOWN_K[1] * P)))

                def down(i, n, last):
                    size = (KD * P, KD * P) if last else (DOWN_K[0] * P, DOWN_K[1] * P)
                    for m in range(2):
                        split_hi(unit(ud + 2 * n + 2 + m, 4, i), n=size[m])
                    if half == 1:
                        w, a = unit(jd + n, 2, i)
                        c = 2 * i + n
                        act.wait_ge(acc_free[a], w + 1)
                        act.wait_ge(sq_added, ADDED_X1 + c)
                        settled()
                        nc.scalar.activation(tb[:, :], wide[:, span(c, 1), :].rearrange("p a n -> p (a n)"),
                                             ACT.Square).then_inc(sq_ready, 1)

                with act.Fori(0, KD // 2 - 1) as i:
                    down(i, 0, False)
                    down(i, 1, False)
                down(KD // 2 - 1, 0, False)
                down(KD // 2 - 1, 1, True)
            row_factor(3)
            split_hi(unit(U_PG + 1))
            split_res(1, None)

            def y_rows_out(c):
                n = c % 2
                act.wait_ge(y_t, c + 1)
                wait(act, y_out[n], 32 * (c // 2))
                nc.scalar.activation(y_row[:, n, 0:RT - 1, :],
                                     small[:, 1024 * n:1024 * n + 512].rearrange("p (r n) -> p r n", n=P), ACT.Copy)
                nc.scalar.activation(y_row[0:DEC, n, RT - 1, :], small[0:DEC, 1024 * n + SEQ:1024 * n + SEQ + P],
                                     ACT.Copy).then_inc(y_rows, 1)

            for c in range(KD):
                _, a = unit(J_PG + c)
                if c < KD - 2:
                    split_hi(unit(U_PG + 2 + c))
                act.wait_ge(unit_done, U_PG + 1 + c)
                wait(act, y_ready, c)
                nc.scalar.activation(halves(tb[:, :]), acc_of(a), ACT.Sigmoid).then_inc(acc_free[a], 1)
                if c >= 2:
                    y_rows_out(c - 2)
            y_rows_out(KD - 2)
            y_rows_out(KD - 1)

        @block.vector
        def _(dve):
            def settled():
                dve.sem_inc(dve_passed, 1)

            def split_lo(vs, n=KD * P):
                v, s = vs
                dve.wait_ge(hi_ready, 2 * v + s + 1)
                nc.vector.tensor_tensor(wlo[:, s, 0:n], raw[:, s, 0:n], whi[:, s, 0:n].bitcast(F32),
                                        ALU.subtract).then_inc(lo_ready, 1)

            def row_factor(n, src, done):
                dve.wait_ge(done[0], done[1])
                nc.vector.tensor_scalar(rowvar[:, 0:RT], src, 1.0 / D, EPS, ALU.mult, ALU.add).then_inc(var_ready, 1)
                dve.wait_ge(rstd_ready, n + 1)
                for r in range(RT):
                    size = P if r < RT - 1 else DEC
                    nc.vector.tensor_scalar(diag[0:size, P * r:P * r + size], ident[0:size, 0:size],
                                            rstd[0:size, r:r + 1], None, ALU.mult).then_inc(diag_ready, 1)

            nc.vector.memset(ones[:, :], 1.0)
            nc.vector.memset(neg_half[:, :], -0.5)
            nc.vector.memset(zeros[:, :], 0.0)
            nc.vector.memset(rowsum[:, :], 0.0).then_inc(init_done, 1)
            dve.wait_ge(gain_t, 1)
            nc.vector.tensor_copy(gains[:, 0:KD], small[:, 1536:1536 + KD]).then_inc(gain_ready, 1)
            dve.wait_ge(gain_ready, 1)
            for k in range(KD + 1):
                if k < KD:
                    dve.wait_ge(xt_psum, k + 1)
                    nc.vector.tensor_copy(x_t[:, k, :], small[:, 1024 * (k % 2):1024 * (k % 2) + ROWS]).then_inc(xt_copied, 1)
                if k > 0:
                    dve.wait_ge(xt_copied, k)
                    dve.wait_ge(xh_ready, k)
                    nc.vector.scalar_tensor_tensor(xl[:, k - 1, :], x_t[:, k - 1, :], gains[:, k - 1:k],
                                                   xh[:, k - 1, :].bitcast(F32), ALU.mult, ALU.subtract).then_inc(xl_ready, 1)
                if k in (2, 5):
                    split_lo(unit(k // 5))
            row_factor(0, rowsum[:, 0:RT], (squares_ready, RT))

            def scaled_out(dst, w, a, u):
                dve.wait_ge(unit_done, u + 1)
                nc.vector.tensor_tensor(halves(dst), acc_of(a), halves(rb[:, :]), ALU.mult).then_inc(acc_free[a], 1)

            for n in range(2):
                split_lo(unit(U_Q + n))
                dve.wait_ge(rb_ready, 1)
                dve.wait_ge(unit_done, n + 1)
                if n == 1:
                    vt_tmp = prob[:, 0:3, :].rearrange("p j n -> p (j n)")[:, 0:ROWS]
                nc.vector.tensor_tensor(halves(kt[:, P:P + ROWS] if n == 0 else vt_tmp), acc_of(n), halves(rb[:, :]),
                                        ALU.mult).then_inc(acc_free[n], 1)
            dve.wait_ge(acc_free[1], 1)
            dve.wait_ge(acc_free[0], 1)
            nc.vector.memset(kt[:, P + ROWS:P + PADROWS], 0.0)
            nc.vector.memset(kt[:, 0:P], 0.0).then_inc(kt_ready, 1)
            nc.vector.memset(va[:, 0, :], 0.0)
            nc.vector.memset(va[64:128, RT, :], 0.0).then_inc(va_ready, 1)
            nc.vector.memset(qt[:, :, ROWS:PADROWS], 0.0)
            nc.vector.memset(qr[:, :, ROWS:PADROWS], 0.0)
            nc.vector.memset(kr[:, :, ROWS:PADROWS], 0.0)
            nc.vector.memset(vr[64:128, :, RT - 1, :], 0.0).then_inc(init_done, 1)
            for k in range(KP):
                dve.wait_ge(xt_psum, KD + k + 1)
                if k == 1:
                    dve.wait_ge(bcast_done, RT)
                nc.vector.tensor_copy((ta, tb)[k][:, :], small[:, 1024 * (k % 2):1024 * (k % 2) + ROWS]).then_inc(xt_copied, 1)
            for k in range(KP):
                dve.wait_ge(xt_copied, KD + k + 1)
                dve.wait_ge(ph_ready, k + 1)
                nc.vector.tensor_tensor(pl[:, k, :], (ta, tb)[k][:, :], ph[:, k, :].bitcast(F32),
                                        ALU.subtract).then_inc(pl_ready, 1)

            def q_out(n):
                w, a = unit(J_Q + n)
                scaled_out(qt[:, n, 0:ROWS], w, a, U_Q + n)

            q_out(0)
            split_lo(unit(U_Q + 2))
            q_out(1)
            split_lo(unit(U_Q + 3))
            dve.wait_ge(kv_t, 1)
            nc.vector.tensor_copy(va[:, 1:RT, :], att[:, 0:512].rearrange("p (r n) -> p r n", n=P)).then_inc(va_rows, 1)
            nc.vector.tensor_copy(gains[:, KD:4 * KD], small[:, 1664 + KD:1664 + 4 * KD])
            nc.vector.tensor_copy(sinks[:, :], small[:, 1728:1728 + HEADS]).then_inc(sinks_ready, 1)
            nc.vector.tensor_copy(ckt[:, :], small[:, 1536:1664]).then_inc(ckt_ready, 1)
            q_out(2)
            split_lo(unit(U_HEAD))
            q_out(3)
            split_lo(unit(U_HEAD + 1))
            dve.wait_ge(sinks_ready, 1)
            dve.wait_ge(tables_in, 32)

            def att_piece(piece, g, b):
                n = 2 * b + g
                nq, k0, k1, tiles = block_size(b)
                if piece == "A":
                    dve.wait_ge(att_score, n + 1)
                    settled()
                    mask = 0 if isinstance(b, int) and b == 0 else (2 if isinstance(b, int) and b == RH else 1)
                    mcol = tab[0:nq, T_MASK + mask * KW + k0:T_MASK + mask * KW + k1]
                    for j in range(GROUP):
                        nc.vector.tensor_tensor_reduce(
                            out=prob[0:nq, j, k0:k1], in0=att[0:nq, j * KW + k0:j * KW + k1], in1=mcol, scale=SCALE,
                            scalar=sinks[0:nq, GROUP * g + j:GROUP * g + j + 1], op0=ALU.add, op1=ALU.max,
                            accum_out=top[0:nq, j:j + 1]).then_inc(dve_top, 1)
                    dve.wait_ge(dve_top, 6 * n + 4)
                    nc.vector.tensor_scalar(neg_top[0:nq, :], top[0:nq, :], -1.0, None, ALU.mult).then_inc(dve_top, 1)
                    dve.wait_ge(dve_top, 6 * n + 5)
                    nc.vector.tensor_tensor(top[0:nq, :], sinks[0:nq, GROUP * g:GROUP * (g + 1)], neg_top[0:nq, :],
                                            ALU.add).then_inc(att_top, 1)
                elif piece == "N":
                    dve.wait_ge(att_exp, n + 1)
                    nc.vector.tensor_tensor(den[0:nq, :], den[0:nq, :], sink_exp[0:nq, :], ALU.add).then_inc(dve_top, 1)
                    dve.wait_ge(dve_top, 6 * n + 6)
                    nc.vector.reciprocal(den[0:nq, :], den[0:nq, :]).then_inc(att_den, 1)
                    dve.wait_ge(att_den, n + 1)
                    for j in range(GROUP):
                        ins = nc.vector.tensor_scalar(prob[0:nq, j, k0:k1], prob[0:nq, j, k0:k1], den[0:nq, j:j + 1], None,
                                                      ALU.mult)
                    ins.then_inc(att_prob, 1)
                elif piece == "B":
                    dve.wait_ge(att_t, n + 1)
                    nc.vector.tensor_copy(prob_t[0:tiles[1], 1, 0:GROUP * nq], att[0:tiles[1], 512:512 + GROUP * nq]).then_inc(att_t1, 1)

            def row_tile(c):
                return (c * P, P if c < RT - 1 else DEC)

            def ret_piece(piece, c, r, slot):
                n = 5 * r + c
                at, size = row_tile(c)
                if piece == "A":
                    dve.wait_ge(ret_B, n + 1 + CREDIT - earlier_use(c))
                    q = qr[:, span(slot, 1), c * P:(c + 1) * P].rearrange("p a n -> p (a n)")
                    nc.vector.tensor_tensor(q_dec[:, c % 2, :], q, tab[:, span(T_QD + P * r, P)], ALU.mult).then_inc(ret_qd, 1)
                    dve.wait_ge(ret_A, n + 1 + CREDIT)
                    nc.vector.tensor_tensor(s_dec[:, c % 2, :], ret_s, tab[:, span(T_DEC + P * r, P)], ALU.mult).then_inc(ret_sd, 1)
                    nc.vector.tensor_scalar(k_dec[:, c % 2, :], ret_kt, tab[:, span((T_KDS if c == RT - 1 else T_KD) + r, 1)],
                                            None, ALU.mult).then_inc(ret_kd, 1)
                elif piece == "B":
                    dve.wait_ge(ret_B, n + 1 + CREDIT)
                    if c == 0:
                        dve.wait_ge(state_p_out, 16 * (r + CREDIT))
                        nc.vector.tensor_scalar(state_p[:, :], ret_dl, 1.0, None, ALU.mult).then_inc(ret_state, 1)
                    else:
                        st, gl = (state_s, T_GLS) if c == RT - 1 else (state_p, T_GL)
                        nc.vector.scalar_tensor_tensor(st[:, :], st[:, :], tab[:, span(gl + r, 1)], ret_dl,
                                                       ALU.mult, ALU.add).then_inc(ret_state, 1)
                    nc.vector.bn_stats(stats[:, 0:6], ret_o).then_inc(dve_ret, 1)
                    dve.wait_ge(dve_ret, 2 * n + 1)
                    settled()
                    nc.vector.bn_aggr(moments[:, :], stats[:, 0:6]).then_inc(dve_ret, 1)
                    dve.wait_ge(dve_ret, 2 * n + 2)
                    nc.vector.tensor_scalar(grstd[:, :], moments[:, 1:2], GN_EPS, None, ALU.add).then_inc(ret_mom, 1)
                elif piece == "N":
                    dve.wait_ge(ret_grstd, n + 1 + CREDIT)
                    dve.wait_ge(ret_C, n + 1 + CREDIT - earlier_use(c))
                    nc.vector.tensor_scalar(o_norm[:, c % 2, :], ret_o, moments[:, 0:1], grstd[:, 0:1],
                                            ALU.subtract, ALU.mult).then_inc(ret_norm, 1)
                elif piece == "C":
                    dve.wait_ge(ret_C, n + 1 + CREDIT)
                    dve.wait_ge(g_ready, 2 * r + 2)
                    dst = o_ret[:, span(EV * r, EV), at:at + size]
                    src = ret_ot.rearrange("p (e n) -> p e n", e=EV)[:, :, 0:size]
                    gate = gr[:, span(slot, 1), :, at:at + size].rearrange("p a e n -> p (a e) n")
                    nc.vector.tensor_tensor(dst, src, gate, ALU.mult).then_inc(ret_gated, 1)

            def job_out(t, h):
                w, a = unit(J_HEAD + t, 6, h)
                if t in (1, 3):
                    wait(dve, g_ready, 2 * h + t // 3)
                scaled_out(zt[:, a, :], w, a, U_HEAD + t + 6 * h)

            def rotate(t, h, slot):
                m = 2 * h + t // 2
                dve.wait_ge(swap_ready, m + 1)
                nc.vector.tensor_tensor(tb[:, :], tb[:, :], rot[:, 1, :], ALU.mult).then_inc(dve_rot, 1)
                dve.wait_ge(dve_rot, m + 1)
                dve.wait_ge(cos_ready, m + 1)
                if not isinstance(h, int):
                    dve.wait_ge(ret_A, 5 * (h - 1) + CREDIT)
                    dve.wait_ge(ret_kst, 5 * (h - 1) + CREDIT)
                dst = (qr if t == 0 else kr)[:, span(slot, 1), 0:ROWS].rearrange("p a n -> p (a n)")
                nc.vector.tensor_tensor(dst, ta[:, :], tb[:, :], ALU.add).then_inc(rotated, 1)

            def v_out(e, h, slot):
                dve.wait_ge(v_t, 2 * h + e + 1)
                if not isinstance(h, int):
                    dve.wait_ge(ret_B, 5 * (h - 1) + CREDIT)
                dst = vr[:, span(slot, 1), :, e * P:(e + 1) * P].rearrange("p a r n -> p (a r) n")
                nc.vector.tensor_scalar(dst[:, 0:RT - 1, :], att[:, 0:512].rearrange("p (r n) -> p r n", n=P), 1.0, None,
                                        ALU.mult)
                nc.vector.tensor_scalar(dst[0:DEC, RT - 1, :], att[0:DEC, SEQ:SEQ + P], 1.0, None,
                                        ALU.mult).then_inc(v_rows, 1)

            def pieces(place, h, b, r, slot, rslot):
                for kind, piece, c in PLACES[place]:
                    if kind == "att":
                        att_piece(piece, c, b)
                    elif kind == "ret" and r is not None:
                        ret_piece(piece, c, r, rslot)
                    elif kind == "v" and h is not None:
                        v_out(c, h, slot)

            def head(h, b, r, slot, rslot):
                for t in range(6):
                    pieces(2 * t, h, b, r, slot, rslot)
                    job_out(t, h)
                    pieces(2 * t + 1, h, b, r, slot, rslot)
                    split_lo(unit(U_HEAD + t + 2, 6, h))
                    if t in (0, 2):
                        rotate(t, h, slot)

            head(0, 0, None, 0, None)
            with dve.Fori(1, RH) as h:
                head(h, h, h - 1, h % 2, (h - 1) % 2)

            def branch_parts(tiles):
                for k in tiles:
                    dst, hi, src = (al[:, k, :], ah[:, k, :], o_att[:, k, :]) if k < GROUP else \
                        (rl[:, k - GROUP, :], rh[:, k - GROUP, :], o_ret[:, k - GROUP, :])
                    dve.wait_ge(branch_hi, k + 1)
                    nc.vector.tensor_tensor(dst, src, hi.bitcast(F32), ALU.subtract).then_inc(branch_lo, 1)

            for t in range(8):
                if t < 6:
                    pieces(2 * t, None, RH, RH - 1, None, (RH - 1) % 2)
                w, a = unit(J_GATE + t)
                if t == 1:
                    dve.wait_ge(g_ready, 2 * RH)
                wait(dve, gate_sig[a], t // 2)
                scaled_out(zt[:, a, :], w, a, U_GATE + t)
                if t < 6:
                    pieces(2 * t + 1, None, RH, RH - 1, None, (RH - 1) % 2)
                split_lo(unit(U_GATE + t + 2) if t < 6 else unit(U_MRG + t - 6), n=(GROUP if t == 6 else KD) * P)
                if t >= 5:
                    branch_parts(range(BRANCH_TILES[t - 5], BRANCH_TILES[t - 4]))
            def gated(u, j, per, c, n, slot, col):
                w, a = unit(j + n, per, c)
                dve.wait_ge(unit_done, u + n + 1 + per * c)
                dve.wait_ge(gate_sig[n], col + 1)
                gate = sig[:, span(slot, 1), n, :].rearrange("p a (h n) -> p (a h) n", h=2)
                nc.vector.tensor_tensor(halves((tb, mb)[n][:, :]), acc_of(a), gate, ALU.mult).then_inc(acc_free[a], 1)

            def merge_sum(c, w1, a1):
                dve.wait_ge(acc_free[a1], w1 + 1)
                wait(dve, m_lo, c)
                nc.vector.tensor_tensor(ta[:, :], tb[:, :], mb[:, :], ALU.add).then_inc(m_ready, 1)

            def merged_lo(c):
                dve.wait_ge(m_hi, c + 1)
                dst = ml[:, span(c, 1), :].rearrange("p a n -> p (a n)")
                hi = yh[:, span(c, 1), :].bitcast(F32).rearrange("p a n -> p (a n)")
                nc.vector.tensor_tensor(dst, ta[:, :], hi, ALU.subtract).then_inc(m_lo, 1)

            def merge_first(c):
                for n in range(4):
                    split_lo(unit(U_MRG + n + 2, 4, c), n=(GROUP if n == 2 else KD) * P)
                    if n < 2:
                        gated(U_MRG, J_MRG, 4, c, n, c, c)
                        if n == 1:
                            w1, a1 = unit(J_MRG + 1, 4, c)
                            merge_sum(c, w1, a1)
                    else:
                        if n == 2:
                            merged_lo(c)
                        w, a = unit(J_MRG + n, 4, c)
                        dve.wait_ge(gate_sig[a], 4 + c)
                        scaled_out(zt[:, a, :], w, a, U_MRG + n + 4 * c)

            dve.wait_ge(branch_lo, GROUP + KD)
            merge_first(0)
            with dve.Fori(1, 4) as c:
                merge_first(c)

            def merge_second(c, last):
                split_lo(unit(U_MRG2 + 2, 2, c), n=(KD if last else GROUP) * P)
                gated(U_MRG2, J_MRG2, 2, c, 0, c, c + 4)
                split_lo(unit(U_MRG2 + 3, 2, c))
                gated(U_MRG2, J_MRG2, 2, c, 1, c, c + 4)
                w1, a1 = unit(J_MRG2 + 1, 2, c)
                merge_sum(c + 4, w1, a1)
                merged_lo(c + 4)

            with dve.Fori(0, 3) as c:
                merge_second(c, False)
            merge_second(3, True)
            with dve.Fori(0, KD // 2) as i:
                for n in range(2):
                    split_lo(unit(U_OUT + 2 + n, 2, i))

            def proj_out(u, j, n, tiles):
                for c in tiles:
                    w, a = unit(j + c)
                    if c < 3:
                        dve.wait_ge(ple_done, 3 * n + c + 1)
                    else:
                        dve.wait_ge(unit_done, u + 1)
                    nc.vector.tensor_copy(halves(proj[:, 4 * n + c, :]), acc_of(a)).then_inc(acc_free[a], 1)

            proj_out(U_P0, J_P0, 0, (0, 1))
            row_factor(1, ret_s[:, 0:RT], (sums_done, 1))
            proj_out(U_P0, J_P0, 0, (2,))

            def new_res(m, k, gain):
                if not (isinstance(k, int) and k == 0):
                    dve.wait_ge(scaled, (KD - 1) * m + k)
                if m == 0:
                    dve.wait_ge(x_back, 16 * KD)
                src = wide[:, span(k, 1), :].rearrange("p a n -> p (a n)")
                dst = res[:, span(k, 1), :].rearrange("p a n -> p (a n)")
                nc.vector.scalar_tensor_tensor(dst, src, gains[:, span(gain + k, 1)], dst, ALU.mult,
                                               ALU.add).then_inc(res_ready, 1)

            def res_lo(m, k, gain):
                dve.wait_ge(y_hi, KD * m + k + 1)
                src = res[:, span(k, 1), :].rearrange("p a n -> p (a n)")
                hi = yh[:, span(k, 1), :].bitcast(F32).rearrange("p a n -> p (a n)")
                dst = yl[:, span(k, 1), :].rearrange("p a n -> p (a n)")
                if gain is None:
                    nc.vector.tensor_tensor(dst, src, hi, ALU.subtract).then_inc(y_lo, 1)
                else:
                    nc.vector.scalar_tensor_tensor(dst, src, gains[:, span(gain + k, 1)], hi, ALU.mult,
                                                   ALU.subtract).then_inc(y_lo, 1)

            def residual(m, g_post, g_next, proj_unit, proj_job, second_unit):
                dve.wait_ge(rb_ready, 2 * m + 2)
                nc.vector.tensor_tensor(wide[:, 0, :], wide[:, 0, :], rb[:, :], ALU.mult).then_inc(first_scaled, 1)
                dve.wait_ge(first_scaled, m + 1)
                new_res(m, 0, g_post)
                new_res(m, 1, g_post)
                res_lo(m, 0, g_next)
                new_res(m, 2, g_post)
                res_lo(m, 1, g_next)
                proj_out(proj_unit, proj_job, m, (3,))
                split_lo(unit(second_unit))
                with dve.Fori(3, KD) as k:
                    new_res(m, k, g_post)
                    res_lo(m, k - 1, g_next)
                res_lo(m, KD - 1, g_next)

            residual(0, KD, 2 * KD, U_P0, J_P0, U_FA + 1)

            def pair_squares(n):
                k = KD // 2 + 2 * n
                dve.wait_ge(sq_ready, k + 2)
                nc.vector.tensor_tensor(sq_x1[:, k, :], sq_x1[:, k, :], sq_x1[:, k + 1, :], ALU.add).then_inc(sq_paired, 1)

            for n in range(2):
                pair_squares(n)
                dve.wait_ge(unit_done, U_FA + n + 1)
                w, a = unit(J_FA + n)
                nc.vector.tensor_copy(halves(zt[:, a, :]), acc_of(a)).then_inc(acc_free[a], 1)
                split_lo(unit(U_FA + 2 + n))
            row_factor(2, ret_s[:, 0:RT], (sums_done, 2))
            dve.wait_ge(rb_ready, 3)
            for n in range(2):
                w, a = unit(J_FA + n)
                dve.wait_ge(acc_free[a], w + 1)
                nc.vector.tensor_tensor(zt[:, a, :], zt[:, a, :], rb[:, :], ALU.mult).then_inc(parked_scaled, 1)
            split_lo(unit(U_FA + 4))
            for half, (uf, jf, ud, jd) in enumerate(((U_FA, J_FA, U_DA, J_DA), (U_FB, J_FB, U_DB, J_DB))):
                def ffn(i, ahead):
                    if half == 0 and isinstance(i, int) and i == 0:
                        a = unit(jf + 1, 2, i)[1]
                        dve.wait_ge(parked_scaled, 2)
                    else:
                        if ahead[0] is not None:
                            split_lo(*ahead[0])
                        w, a = unit(jf, 2, i)
                        dve.wait_ge(rb_ready, 3)
                        scaled_out(zt[:, a, :], w, a, uf + 2 * i)
                        split_lo(*ahead[1])
                        w, a = unit(jf + 1, 2, i)
                        scaled_out(zt[:, a, :], w, a, uf + 1 + 2 * i)
                        dve.wait_ge(acc_free[a], w + 1)
                    dve.wait_ge(silu_ready, half * FTH + i + 1)
                    nc.vector.tensor_tensor(ta[:, :], ta[:, :], zt[:, a, :], ALU.mult).then_inc(f_ready, 1)
                    dve.wait_ge(f_hi, half * FTH + i + 1)
                    dst = fl[:, span(i, 1), :].rearrange("p a n -> p (a n)")
                    hi = fh[:, span(i, 1), :].bitcast(F32).rearrange("p a n -> p (a n)")
                    nc.vector.tensor_tensor(dst, ta[:, :], hi, ALU.subtract).then_inc(f_lo, 1)

                if half == 0:
                    ffn(0, (None, None))
                    ffn(1, (None, (unit(uf + 5),)))
                with dve.Fori(2 * (1 - half), FTH - 1) as i:
                    ffn(i, ((unit(uf + 2, 2, i),), (unit(uf + 3, 2, i),)))
                ffn(FTH - 1, ((unit(ud), DOWN_K[0] * P), (unit(ud + 1), DOWN_K[1] * P)))

                def down(i, n, last):
                    size = (KD * P, KD * P) if last else (DOWN_K[0] * P, DOWN_K[1] * P)
                    split_lo(unit(ud + 2 * n + 2, 4, i), n=size[0])
                    w, a = unit(jd + n, 2, i)
                    c = 2 * i + n
                    dve.wait_ge(unit_done, ud + 2 + 2 * c)
                    dst = wide[:, span(c, 1), :].rearrange("p a (h n) -> p (a h) n", h=2)
                    if half == 0:
                        nc.vector.tensor_scalar(dst, acc_of(a), 1.0, None, ALU.mult).then_inc(acc_free[a], 1)
                    else:
                        nc.vector.tensor_tensor(dst, acc_of(a), dst, ALU.add).then_inc(acc_free[a], 1)
                    split_lo(unit(ud + 2 * n + 3, 4, i), n=size[1])

                with dve.Fori(0, KD // 2 - 1) as i:
                    down(i, 0, False)
                    down(i, 1, False)
                down(KD // 2 - 1, 0, False)
                down(KD // 2 - 1, 1, True)
            proj_out(U_P1, J_P1, 1, (0, 1))
            row_factor(3, ret_s[:, 0:RT], (sums_done, 3))
            proj_out(U_P1, J_P1, 1, (2,))
            residual(1, 3 * KD, None, U_P1, J_P1, U_PG + 1)

            def y_piece(i, n, ahead):
                w, a = unit(J_PG + n, 2, i)
                c = 2 * i + n
                if ahead:
                    split_lo(unit(U_PG + 2 + n, 2, i))
                dve.wait_ge(acc_free[a], w + 1)
                wait(dve, y_t, c - 1)
                nc.vector.tensor_tensor(yt[:, n, :], tb[:, :], proj[:, span(c, 1), :].rearrange("p a n -> p (a n)"),
                                        ALU.mult).then_inc(dve_y, 1)
                dve.wait_ge(dve_y, c + 1)
                nc.vector.tensor_tensor(yt[:, n, :], yt[:, n, :], res[:, span(c, 1), :].rearrange("p a n -> p (a n)"),
                                        ALU.add).then_inc(y_ready, 1)

            for c in range(KD):
                y_piece(c // 2, c % 2, c < KD - 2)

        @block.gpsimd
        def _(pool):
            def settled():
                pool.sem_inc(pool_passed, 1)

            for s_ in (ret_kst, ret_qd, ret_A, ret_sd, ret_kd, ret_B, ret_state, ret_grstd, ret_norm, ret_C,
                       ret_gated):
                pool.sem_inc(s_, CREDIT)
            pool.sem_inc(y_rows, Y_CREDIT)

            def power(n):
                pool.wait_ge(var_ready, n + 1)
                nc.gpsimd.tensor_tensor(rstd[:, 0:RT], rowvar[:, 0:RT], neg_half[:, 0:RT], ALU.pow).then_inc(rstd_ready, 1)

            for n, g in ((1, g_mix_post), (2, g_ffn_pre), (3, g_ffn_post)):
                pool.dma_start(g_row[n * KD:(n + 1) * KD, :], g[0].rearrange("(k p) -> k p", p=P)).then_inc(gains_in, 16)
            pool.dma_start(sink_row[:, :], sinks_in).then_inc(gains_in, 16)
            power(0)
            pool.dma_start(p_row[:, 0:RT - 1, :], p_p[0, 0].rearrange("(r p) n -> p r n", p=P)).then_inc(p_in, 16)
            pool.dma_start(p_row[0:DEC, RT - 1, :], p_s[0, 0]).then_inc(p_in, 16)
            pool.dma_start(ck_row[:, :], cache_k[0, 0].rearrange("n h d -> n (h d)")).then_inc(cache_in, 16)
            pool.dma_start(cva[:, :], cache_v[0, 0].rearrange("n h d -> n (h d)")).then_inc(cache_in, 16)
            pool.dma_start(tab[:, T_ID + P:T_COLS], table_in[:, T_ID + P:T_COLS]).then_inc(tables_in, 16)
            pool.dma_start(rot[:, :, :], table_in[:, T_ROT:T_ALL].rearrange("p (a n) -> p a n", a=2)).then_inc(tables_in, 16)
            pool.wait_ge(xt_copied, KD)
            pool.dma_start(scratch, x_t[:, :, :].rearrange("p k n -> p (k n)")).then_inc(x_saved, 16)
            pool.wait_ge(kv_rows, 1)
            pool.wait_ge(va_rows, 2)

            def stage_block(b):
                if isinstance(b, int) and b == 0:
                    pool.wait_ge(kt_ready, 1)
                    nc.gpsimd.tensor_copy(k_st[:, :], kt[:, 0:KW])
                    nc.gpsimd.tensor_copy(v_st[:, :, :], va[:, 0:2, :])
                    pool.wait_ge(init_done, 2)
                    pool.wait_ge(acc_free[0], J_HEAD // 2)
                    pool.wait_ge(acc_free[1], J_HEAD // 2)
                    nc.gpsimd.tensor_copy(q_st[:, :, :], qt[:, :, 0:P]).then_inc(att_staged, 1)
                else:
                    pool.wait_ge(att_pv, 2 * b)
                    settled()
                    nc.gpsimd.tensor_copy(k_st[:, :], kt[:, span(P * b, KW)])
                    nc.gpsimd.tensor_copy(v_st[:, :, :], va[:, span(b, 2), :])
                    nc.gpsimd.tensor_copy(q_st[:, :, :], qt[:, :, span(P * b, P)]).then_inc(att_staged, 1)

            def stage_k(c, r, slot):
                pool.wait_ge(ret_A, 5 * r + max(0, c - 1) + CREDIT)
                pool.wait_ge(rotated, 2 * r + 2)
                settled()
                nc.gpsimd.tensor_copy(rk_st[:, c % 2, :], kr[:, span(slot, 1), c * P:(c + 1) * P].rearrange(
                    "p a n -> p (a n)")).then_inc(ret_kst, 1)

            def ret_piece(piece, c, r, slot):
                n = 5 * r + c
                if piece == "A" and c < RT - 1:
                    stage_k(c + 1, r, slot)
                elif piece == "B":
                    pool.wait_ge(ret_mom, n + 1)
                    nc.gpsimd.tensor_tensor(grstd[:, :], grstd[:, :], neg_half[:, 0:1], ALU.pow).then_inc(ret_grstd, 1)

            def head_job(t, h, slot):
                w, a = unit(J_HEAD + t, 6, h)
                if t in (0, 2):
                    m = 2 * h + t // 2
                    pool.wait_ge(acc_free[a], w + 1)
                    wait(pool, rotated, m)
                    nc.gpsimd.tensor_tensor(ta[:, :], zt[:, a, :], rot[:, 0, :], ALU.mult).then_inc(cos_ready, 1)
                elif t in (1, 5):
                    m = 2 * h + t // 5
                    pool.wait_ge(sg_ready, m + 1)
                    if not isinstance(h, int):
                        pool.wait_ge(ret_gated, 5 * (h - 1) + CREDIT)
                    settled()
                    nc.gpsimd.tensor_tensor(gr[:, span(slot, 1), t // 5, :].rearrange("p a n -> p (a n)"),
                                            zt[:, a, :], tb[:, :], ALU.mult).then_inc(g_ready, 1)

            def pieces(place, r, rslot):
                for kind, piece, c in PLACES[place]:
                    if kind == "ret" and r is not None:
                        ret_piece(piece, c, r, rslot)

            def head(h, r, slot, rslot):
                for t in range(6):
                    pieces(2 * t, r, rslot)
                    if t == 5:
                        stage_block(h + 1)
                        stage_k(0, h, slot)
                    head_job(t, h, slot)
                    pieces(2 * t + 1, r, rslot)

            stage_block(0)
            half_rows = lambda ap: ap[0, 0].rearrange("n h d -> n (h d)")
            pool.dma_start(half_rows(k_p), k_row[:, 0, :]).then_inc(out_done, 16)
            pool.dma_start(half_rows(v_p), va[:, RT - 1, :]).then_inc(out_done, 16)
            pool.dma_start(half_rows(k_s)[DEC:P, :], k_row[0:DEC, 1, :]).then_inc(out_done, 16)
            pool.dma_start(half_rows(v_s)[DEC:P, :], va[0:DEC, RT, :]).then_inc(out_done, 16)
            pool.dma_start(half_rows(k_s)[0:DEC, :], half_rows(cache_k)[DEC:P, :]).then_inc(out_done, 16)
            pool.dma_start(half_rows(v_s)[0:DEC, :], half_rows(cache_v)[DEC:P, :]).then_inc(out_done, 16)
            pool.wait_ge(tables_in, 32)
            head(0, None, 0, None)
            with pool.Fori(1, RH) as h:
                head(h, h - 1, h % 2, (h - 1) % 2)
            for place_ in range(12):
                pieces(place_, RH - 1, (RH - 1) % 2)
            pool.wait_ge(unit_done, U_MRG2)
            pool.wait_ge(x_saved, 16)
            for k in range(KD):
                pool.dma_start(res[:, k, :], scratch[:, k * ROWS:(k + 1) * ROWS]).then_inc(x_back, 16)
            pool.wait_ge(unit_done, U_OUT)
            nc.gpsimd.memset(sqacc[:, ROWS:PADROWS], 0.0)

            def add_square(src, m, fresh):
                if fresh:
                    wait(pool, sums_done, 2 if m else 0)
                    nc.gpsimd.tensor_copy(sqacc[:, 0:ROWS], src[:, :]).then_inc(sq_added, 1)
                else:
                    pool.wait_ge(sq_added, m)
                    nc.gpsimd.tensor_tensor(sqacc[:, 0:ROWS], sqacc[:, 0:ROWS], src[:, :], ALU.add).then_inc(sq_added, 1)

            def out_square(i, n, fresh=False):
                w, a = unit(J_OUT + n, 2, i)
                pool.wait_ge(acc_free[a], w + 1)
                add_square(tb, 2 * i + n, fresh)

            out_square(0, 0, fresh=True)
            out_square(0, 1)
            with pool.Fori(1, KD // 2) as i:
                out_square(i, 0)
                out_square(i, 1)
            power(1)

            pool.wait_ge(rb_ready, 2)
            def scale_tile(k):
                ap = wide[:, span(k, 1), :].rearrange("p a n -> p (a n)")
                nc.gpsimd.tensor_tensor(ap, ap, rb[:, :], ALU.mult).then_inc(scaled, 1)

            with pool.Fori(1, KD) as k:
                scale_tile(k)
            pool.wait_ge(sq_ready, 2)
            nc.gpsimd.tensor_tensor(sqacc[:, 0:ROWS], sq_x1[:, 0, :], sq_x1[:, 1, :], ALU.add).then_inc(sq_added, 1)
            for n, k in enumerate((2, 3, 4, 6)):
                if k < KD // 2:
                    pool.wait_ge(sq_ready, k + 1)
                else:
                    pool.wait_ge(sq_paired, (k - KD // 2) // 2 + 1)
                pool.wait_ge(sq_added, ADDED_OUT + n + 1)
                nc.gpsimd.tensor_tensor(sqacc[:, 0:ROWS], sqacc[:, 0:ROWS], sq_x1[:, k, :], ALU.add).then_inc(sq_added, 1)
            power(2)
            for half, (uf, jf) in enumerate(((U_FA, J_FA), (U_FB, J_FB))):
                def silu(i):
                    m = half * FTH + i
                    pool.wait_ge(silu_sg, m + 1)
                    wait(pool, f_lo, m)
                    nc.gpsimd.tensor_tensor(ta[:, :], zt[:, jf % 2, :], tb[:, :], ALU.mult).then_inc(silu_ready, 1)

                silu(0)
                with pool.Fori(1, FTH) as i:
                    silu(i)
            pool.wait_ge(sq_ready, KD + 1)
            add_square(tb, ADDED_X1, True)
            with pool.Fori(1, KD) as c:
                pool.wait_ge(sq_ready, KD + 1 + c)
                add_square(tb, ADDED_X1 + c, False)
            power(3)
            pool.wait_ge(rb_ready, 4)
            with pool.Fori(1, KD) as k:
                scale_tile(k)
            pool.wait_ge(out_done, 16 * 6)


INPUTS = ["x_prompt", "x_sample", "p_prompt", "p_sample", "cache_attn_k", "cache_attn_v", "state_ret",
          "g_mix_pre", "w_in", "attn_sinks", "w_branch_attn", "w_branch_ret", "w_out", "g_mix_post",
          "g_ffn_pre", "w_ffn_gate", "w_ffn_up", "w_ffn_down", "g_ffn_post", "w_ple_proj", "w_ple_gate"]
OUTPUTS = [(1, SEQ, D), (1, DEC, D), (1, 1, P, KV, HD), (1, 1, P, KV, HD), (1, 1, RH, RK, RV),
           (1, 1, P, KV, HD), (1, 1, P, KV, HD), (1, 1, RH, RK, RV)]


def kernel(**inputs):
    import concourse.bacc as bacc
    from concourse.bass_utils import run_bass_kernel_spmd

    nc = bacc.Bacc("TRN2", target_bir_lowering=False, num_devices=1)
    arrays, args = {}, []
    for name in INPUTS:
        a = np.ascontiguousarray(inputs[name])
        arrays["in_" + name] = a
        args.append(nc.dram_tensor("in_" + name, a.shape, F32, kind="ExternalInput").ap())
    arrays["in_tables"] = tables()
    args.append(nc.dram_tensor("in_tables", (P, T_ALL), F32, kind="ExternalInput").ap())
    args.append(nc.dram_tensor("x_scratch", (P, KD * ROWS), F32, kind="Internal").ap())
    for i, shape in enumerate(OUTPUTS):
        args.append(nc.dram_tensor(f"out_{i}", shape, F32, kind="ExternalOutput").ap())
    encoder_layer(nc, *args)
    r = run_bass_kernel_spmd(nc, [arrays], core_ids=[0])
    return tuple(r.results[0][f"out_{i}"] for i in range(len(OUTPUTS)))
```
